# Optimizing a Trainium2 kernel written in Bass

```python
import math
import jax, jax.numpy as jnp
from jax import lax
import numpy as np

D_MODEL = 1024
BATCH = 1
SEQ = 512
DEPTH = 2

D_PLE = 256
D_MIX = D_MODEL
ATTN_WIDTH = D_MIX // 2
N_DIFF_HEADS = 4
DIFF_V_DIM = ATTN_WIDTH // N_DIFF_HEADS
DIFF_QK_DIM = DIFF_V_DIM // 2
CONV_WIDTH = D_MIX - ATTN_WIDTH
N_CONV_GROUPS = 8
CONV_GROUP_DIM = CONV_WIDTH // N_CONV_GROUPS
CONV_K = 3
D_IN = 3 * ATTN_WIDTH + 3 * CONV_WIDTH
D_FF = 2816
Q_BLOCK = 128
EPS = 1e-6

kernel_name = "hymba_diffattn_shortconv_macaron_ple"

def rmsnorm(x, g):
    xf = x.astype(jnp.float32)
    y = xf * lax.rsqrt(jnp.mean(xf * xf, axis=-1, keepdims=True) + EPS)
    return (y * g.astype(jnp.float32)).astype(x.dtype)

def swiglu(x, w_gate, w_up, w_down):
    return (jax.nn.silu(x @ w_gate) * (x @ w_up)) @ w_down

def causal_diff_attention(q, k, v, lam):
    b, s, h, dv = v.shape
    n_blocks = s // Q_BLOCK
    scale = 1.0 / math.sqrt(DIFF_QK_DIM)
    k_pos = jnp.arange(s)

    def block(i):
        start = i * Q_BLOCK
        qb = lax.dynamic_slice_in_dim(q, start, Q_BLOCK, axis=1)
        sc = jnp.einsum('bqhmd,bkhmd->bhmqk', qb, k).astype(jnp.float32) * scale
        q_pos = start + jnp.arange(Q_BLOCK)
        mask = k_pos[None, :] <= q_pos[:, None]
        sc = jnp.where(mask, sc, -jnp.inf)
        a = jax.nn.softmax(sc, axis=-1)
        diff = a[:, :, 0] - lam * a[:, :, 1]
        return jnp.einsum('bhqk,bkhe->bqhe', diff.astype(v.dtype), v)

    out = lax.map(block, jnp.arange(n_blocks))
    return jnp.transpose(out, (1, 0, 2, 3, 4)).reshape(b, s, h, dv)

def causal_dwconv(u, w, bias):
    c = u.shape[-1]
    y = lax.conv_general_dilated(
        u, w[:, None, :].astype(u.dtype), window_strides=(1,),
        padding=[(CONV_K - 1, 0)], dimension_numbers=('NWC', 'WIO', 'NWC'),
        feature_group_count=c)
    return y + bias

def setup_inputs(seed: int = 0) -> dict:
    key = jax.random.key(seed)
    ks = iter(jax.random.split(key, 32))

    def nrm(shape, scale):
        return jax.random.normal(next(ks), shape, jnp.float32) * scale

    def gain(shape):
        return 1.0 + nrm(shape, 0.01)

    return {
        "x": nrm((BATCH, SEQ, D_MODEL), 1.0),
        "p": nrm((DEPTH, BATCH, SEQ, D_PLE), 1.0),
        "ffn1_norm": gain((DEPTH, D_MODEL)),
        "ffn1_w_gate": nrm((DEPTH, D_MODEL, D_FF), D_MODEL ** -0.5),
        "ffn1_w_up": nrm((DEPTH, D_MODEL, D_FF), D_MODEL ** -0.5),
        "ffn1_w_down": nrm((DEPTH, D_FF, D_MODEL), D_FF ** -0.5),
        "mix_norm": gain((DEPTH, D_MODEL)),
        "w_in": nrm((DEPTH, D_MODEL, D_IN), D_MODEL ** -0.5),
        "q_norm": gain((DEPTH, DIFF_QK_DIM)),
        "k_norm": gain((DEPTH, DIFF_QK_DIM)),
        "lambda_q1": nrm((DEPTH, DIFF_QK_DIM), 0.1),
        "lambda_k1": nrm((DEPTH, DIFF_QK_DIM), 0.1),
        "lambda_q2": nrm((DEPTH, DIFF_QK_DIM), 0.1),
        "lambda_k2": nrm((DEPTH, DIFF_QK_DIM), 0.1),
        "attn_out_norm": gain((DEPTH, DIFF_V_DIM)),
        "conv_w": nrm((DEPTH, CONV_K, CONV_WIDTH), CONV_K ** -0.5),
        "conv_b": nrm((DEPTH, CONV_WIDTH), 0.01),
        "conv_out_norm": gain((DEPTH, CONV_WIDTH)),
        "w_out": nrm((DEPTH, D_MIX, D_MODEL), D_MIX ** -0.5),
        "ffn2_norm": gain((DEPTH, D_MODEL)),
        "ffn2_w_gate": nrm((DEPTH, D_MODEL, D_FF), D_MODEL ** -0.5),
        "ffn2_w_up": nrm((DEPTH, D_MODEL, D_FF), D_MODEL ** -0.5),
        "ffn2_w_down": nrm((DEPTH, D_FF, D_MODEL), D_FF ** -0.5),
        "ple_norm": gain((DEPTH, D_MODEL)),
        "ple_w_gate": nrm((DEPTH, D_MODEL, D_MODEL), D_MODEL ** -0.5),
        "ple_w_proj": nrm((DEPTH, D_PLE, D_MODEL), D_PLE ** -0.5),
    }

def reference(x, p, ffn1_norm, ffn1_w_gate, ffn1_w_up, ffn1_w_down,
              mix_norm, w_in, q_norm, k_norm,
              lambda_q1, lambda_k1, lambda_q2, lambda_k2, attn_out_norm,
              conv_w, conv_b, conv_out_norm, w_out,
              ffn2_norm, ffn2_w_gate, ffn2_w_up, ffn2_w_down,
              ple_norm, ple_w_gate, ple_w_proj):
    b, s, _ = x.shape
    splits = [ATTN_WIDTH, 2 * ATTN_WIDTH, 3 * ATTN_WIDTH,
              3 * ATTN_WIDTH + CONV_WIDTH, 3 * ATTN_WIDTH + 2 * CONV_WIDTH]
    for i in range(DEPTH):
        lam_init = 0.8 - 0.6 * math.exp(-0.3 * i)

        x = x + 0.5 * swiglu(rmsnorm(x, ffn1_norm[i]), ffn1_w_gate[i], ffn1_w_up[i], ffn1_w_down[i])

        h = rmsnorm(x, mix_norm[i])
        z = h @ w_in[i]
        q, k, v, g_b, g_c, hc = jnp.split(z, splits, axis=-1)

        q = rmsnorm(q.reshape(b, s, N_DIFF_HEADS, 2, DIFF_QK_DIM), q_norm[i])
        k = rmsnorm(k.reshape(b, s, N_DIFF_HEADS, 2, DIFF_QK_DIM), k_norm[i])
        v = v.reshape(b, s, N_DIFF_HEADS, DIFF_V_DIM)
        lam = (jnp.exp(jnp.sum(lambda_q1[i].astype(jnp.float32) * lambda_k1[i].astype(jnp.float32)))
               - jnp.exp(jnp.sum(lambda_q2[i].astype(jnp.float32) * lambda_k2[i].astype(jnp.float32)))
               + lam_init)
        o = causal_diff_attention(q, k, v, lam)
        o = (rmsnorm(o, attn_out_norm[i]) * (1.0 - lam_init)).reshape(b, s, ATTN_WIDTH)

        yc = g_b * causal_dwconv(g_c * hc, conv_w[i], conv_b[i])
        yc = rmsnorm(yc.reshape(b, s, N_CONV_GROUPS, CONV_GROUP_DIM),
                     conv_out_norm[i].reshape(N_CONV_GROUPS, CONV_GROUP_DIM)).reshape(b, s, CONV_WIDTH)

        x = x + jnp.concatenate([o, yc], axis=-1) @ w_out[i]

        x = x + 0.5 * swiglu(rmsnorm(x, ffn2_norm[i]), ffn2_w_gate[i], ffn2_w_up[i], ffn2_w_down[i])

        gate = jax.nn.sigmoid(rmsnorm(x, ple_norm[i]) @ ple_w_gate[i])
        x = x + gate * (p[i] @ ple_w_proj[i])
    return x


_drawn_inputs = setup_inputs


def setup_inputs(seed=0):
    import zlib

    import numpy as np

    out = dict(_drawn_inputs(seed))
    spreads = {}
    factors = {'ffn1_norm': 7.353,
     'mix_norm': 3.337,
     'q_norm': 8.0,
     'k_norm': 8.0,
     'lambda_k1': 3.253,
     'attn_out_norm': 64.0,
     'conv_b': 57.368,
     'conv_out_norm': 62.807,
     'ffn2_norm': 8.0,
     'ple_norm': 64.0}
    for name, (base, spread) in spreads.items():
        noise = np.random.default_rng([zlib.crc32(name.encode()), seed]).standard_normal(out[name].shape)
        drawn = base * np.exp(spread * noise) if base else spread * noise
        out[name] = __import__('jax').numpy.asarray(drawn.astype(out[name].dtype))
    for name, factor in factors.items():
        out[name] = (out[name] * factor).astype(out[name].dtype)
    return out
```

```python
from contextlib import ExitStack
import math

import numpy as np
import concourse.bass as bass
from concourse import mybir

P = 128
T = 512
D = 1024
KD = D // P
D_FF = 2816
LAYERS = 2
D_PLE = 256
KP = D_PLE // P
HEADS = 4
QK = 64
EPS = 1e-6
PARTS = (12, 10)
assert sum(PARTS) * P == D_FF
PLE_BLOCKS = KD + KP

MIX = ([(k, 0) for k in "qkv"] + [(k, 1) for k in "qkv"] + [(k, 0) for k in "chb"]
       + [(k, 2) for k in "qkv"] + [(k, 1) for k in "chb"] + [(k, 3) for k in "qkv"]
       + [(k, 2) for k in "chb"] + [(k, 3) for k in "chb"])
COLUMN = {"q": 0, "k": 4, "v": 8, "b": 12, "c": 16, "h": 20}

FFN_CHUNKS = sum(2 * f + KD for f in PARTS)
AT_FFN = (0, FFN_CHUNKS + len(MIX) + KD)
AT_MIX = FFN_CHUNKS
AT_OUT = AT_MIX + len(MIX)
AT_PLE = AT_FFN[1] + FFN_CHUNKS
CHUNKS = AT_PLE + KD
RAW = 4
BLOCKS = max(PARTS)

G_FFN1, G_MIX, G_FFN2, G_PLE = (KD * s for s in range(4))
G_Q = 4 * KD
G_K = G_Q + 1
G_O = G_K + 1
G_CB = G_O + 1
G_CN = G_CB + 4
G_CW = G_CN + 4
GAINS = G_CW + 12

RESID = 4
NORMS = RESID + 4 * HEADS


def lambda_init(layer):
    return 0.8 - 0.6 * math.exp(-0.3 * layer)


def mix_hooks():
    places = []

    def put(chunk, block, task, head):
        places.append((chunk, block, len(places), task, head))

    for h in range(HEADS):
        b = MIX.index(("q", h))
        late = h == 0
        put(b + 1 + late, 3 - 3 * late, "q_sum", h)
        put(b + 2, 1 + 3 * late, "q_spread", h)
        put(b + 2, 2 + 3 * late, "k_sum", h)
        put(b + 2 + late, 7 * (1 - late), "k_spread", h)
        put(b + 3, 5, "v_turn", h)
        for i, (c, k) in enumerate([(3, 3), (3, 7), (4, 4), (5, 1)]):
            put(b + c, k, "score", (h, i))
        for i, (c, k) in enumerate([(4, 2), (4, 7), (5, 4), (5, 6)]):
            put(b + c, k, "turn", (h, i))
        put(b + 6, 1, "attend", h)
        put(b + 6, 6, "o_sum", h)
        put(b + 7, 2, "o_spread", h)
        c = MIX.index(("c", h))
        put(c + 3, 3, "c_sum", h)
        put(c + 3, 6, "c_spread", h)
    hooks = {}
    for chunk, block, _, task, head in sorted(places):
        hooks.setdefault(chunk, []).append((block, task, head))
    return hooks


HOOKS = mix_hooks()
_ORDER = [(t[0], h) for c in sorted(HOOKS) for _, t, h in HOOKS[c] if t.endswith("_sum")]
_SPREADS = [(t[0], h) for c in sorted(HOOKS) for _, t, h in HOOKS[c] if t.endswith("_spread")]
assert _ORDER == _SPREADS and len(_ORDER) == 4 * HEADS
NORM_AT = {name: 2 + i for i, name in enumerate(_ORDER)}
RESID_AT = (0, 1, NORMS - 2, NORMS - 1)
Y_AT = {name: i for i, name in enumerate(n for n in _ORDER if n[0] in "oc")}
CONV_STEPS = 4


def build(nc, w_gu, w_down, w_mix, w_out, w_ple, x_in, p_in, vec_in, lam_in, out):
    f32, f32r = mybir.dt.float32, mybir.dt.float32r
    ALU, ACT, AX = mybir.AluOpType, mybir.ActivationFunctionType, mybir.AxisListType

    ctx = ExitStack()
    with ctx:
        def sb(name, cols, dt=f32):
            return ctx.enter_context(nc.sbuf_tensor(name, [P, cols], dt))

        def bank(name, banks=1):
            return ctx.enter_context(nc.psum_tensor(name, [P, banks * T], f32))

        def sem(name):
            return ctx.enter_context(nc.semaphore(name))

        x = sb("x", KD * T)
        h_hi, h_lo = sb("h_hi", KD * T, f32r), sb("h_lo", KD * T, f32r)
        a_hi, a_lo = sb("a_hi", BLOCKS * T, f32r), sb("a_lo", BLOCKS * T, f32r)
        raw = [sb(f"raw{s}", BLOCKS * P) for s in range(RAW)]
        w_hi = [sb(f"w_hi{s}", BLOCKS * P, f32r) for s in range(2)]
        w_lo = [sb(f"w_lo{s}", BLOCKS * P, f32r) for s in range(2)]
        p_hi, p_lo = sb("p_hi", KP * T, f32r), sb("p_lo", KP * T, f32r)
        rstd = sb("rstd", T)
        square_sum = sb("square_sum", T)
        square = sb("square", T)
        square_x = square
        std, inv = sb("std", 8), sb("inv", 8)
        inv_wide = sb("inv_wide", T)
        tmp_a, tmp_b, tmp_c, tmp_d = (sb(f"tmp_{c}", T) for c in "abcd")
        q_t = [sb(f"q_t{s}", T) for s in range(2)]
        k_t = [sb(f"k_t{s}", T) for s in range(2)]
        v_t = sb("v_t", T)
        v_rows = [sb(f"v_rows{s}", T) for s in range(2)]
        exps = sb("exps", 2 * T)
        diff_at = [0, P, 3 * P, 6 * P]
        diff = sb("diff", 10 * P)
        diff_t = sb("diff_t", 4 * T)
        o_t = sb("o_t", T)
        u_pad = sb("u_pad", T + 2)
        row_top, row_max, row_sum, row_inv = (sb(f"row_{s}", 2) for s in ("top", "max", "sum", "inv"))
        ident, causal = sb("ident", P), sb("causal", P)
        ones2, halves = sb("ones2", 2), sb("halves", 2)
        eps = sb("eps", 1)
        vecs, gain = sb("vecs", LAYERS * GAINS), sb("gain", GAINS)
        lam_vecs = diff[:, 0:LAYERS * 4 * QK]
        lam_prod = o_t[:, 0:LAYERS * 2 * QK]
        lam_sum, lam_exp = sb("lam_sum", LAYERS * 2), sb("lam_exp", LAYERS * 2)
        neg_lam, neg_lam_now = sb("neg_lam", LAYERS), sb("neg_lam_now", 1)
        p_raw = exps

        acc = [bank(f"acc{s}") for s in range(2)]
        scores = bank("scores", 2)
        turned = bank("turned")
        values = bank("values")
        sums = bank("sums")
        spread = bank("spread")

        raw_loaded = [sem(f"raw_loaded{s}") for s in range(RAW)]
        x_loaded, consts_loaded, p_loaded, out_stored = (
            sem(s) for s in ("x_loaded", "consts_loaded", "p_loaded", "out_stored"))
        zeroed, consts_ready, setup_step, lam_exp_ready, gain_scaled, gain_ready = (
            sem(s) for s in ("zeroed", "consts_ready", "setup_step", "lam_exp_ready", "gain_scaled", "gain_ready"))
        hi_split = sem("hi_split")
        lo_split = sem("lo_split")
        group_done = sem("group_done")
        drained = sem("drained")
        x_done = sem("x_done")
        h_hi_done, h_lo_done = sem("h_hi_done"), sem("h_lo_done")
        sq_x_done, sq_x_added = sem("sq_x_done"), sem("sq_x_added")
        square_done, sums_done, std_done, inv_done, wide_done, spread_done, norm_used = (
            sem(s) for s in ("square_done", "sums_done", "std_done", "inv_done", "wide_done", "spread_done", "norm_used"))
        silu_done, inner_done, a_hi_done, a_lo_done = (
            sem(s) for s in ("silu_done", "inner_done", "a_hi_done", "a_lo_done"))
        v_turned, v_rows_ready = sem("v_turned"), sem("v_rows_ready")
        scores_done, masked, max_done, max_ready, exp_done, inv_step, diff_step, diff_ready = (
            sem(s) for s in ("scores_done", "masked", "max_done", "max_ready", "exp_done", "inv_step", "diff_step", "diff_ready"))
        turn_done, diff_t_ready, attended, o_ready = (
            sem(s) for s in ("turn_done", "diff_t_ready", "attended", "o_ready"))
        conv_step, conv_done = sem("conv_step"), sem("conv_done")
        y_hi_done, y_lo_done = sem("y_hi_done"), sem("y_lo_done")
        p_hi_done, p_lo_done = sem("p_hi_done"), sem("p_lo_done")
        sigmoid_done, gated = sem("sigmoid_done"), sem("gated")

        def tile(t, k, n=1):
            return t[:, k * T:(k + n) * T]

        def dyn(t, k):
            return t[:, bass.ds(k * T, T)]

        def inner(l, f, part, t):
            return (2 * l + f) * sum(PARTS) + sum(PARTS[:part]) + t

        def ahead(turn, j):
            return (turn, j + 2) if j < 2 else (turn + 1, j - 2)

        block = ctx.enter_context(nc.Block())

        @block.sync
        def _(sp):
            def load(slot, src):
                sp.dma_start(raw[slot][:, 0:src.shape[-1]], src).then_inc(raw_loaded[slot], 16)

            def load_section(l, at, count, source):
                with sp.Fori(0, count // RAW) as i:
                    for j in range(RAW):
                        sp.wait_ge(lo_split, l * CHUNKS + at + RAW * i + j - RAW + 1)
                        load(j, source(RAW * i + j))

            sp.dma_start(vecs[:, :], vec_in).then_inc(consts_loaded, 16)
            sp.dma_start(lam_vecs[:, :], lam_in.partition_broadcast(P)).then_inc(consts_loaded, 16)
            for k in range(KD):
                sp.dma_start(tile(x, k), x_in[:, k * T:(k + 1) * T]).then_inc(x_loaded, 16)
            sp.sem_inc(p_loaded, 16)
            for semaphore in raw_loaded:
                sp.sem_inc(semaphore, 16 * CHUNKS // RAW)
            with sp.Fori(1, LAYERS + 1) as l:
                sp.wait_ge(p_lo_done, l)
                sp.wait_ge(diff_ready, l * 4 * HEADS)
                sp.dma_start(p_raw[:, :], p_in[l - 1, :, :]).then_inc(p_loaded, 16)
                for f in range(2):
                    at, done = AT_FFN[f], 0
                    for part, tiles in enumerate(PARTS):
                        load_section(l, at, 2 * tiles, lambda n: w_gu[l - 1, f, 2 * done + n, :, :])
                        at += 2 * tiles
                        load_section(l, at, KD, lambda n: w_down[part][l - 1, f, n, :, :])
                        at += KD
                        done += tiles
                    if f == 0:
                        load_section(l, AT_MIX, len(MIX), lambda n: w_mix[l - 1, n, :, :])
                        load_section(l, AT_OUT, KD, lambda n: w_out[l - 1, n, :, :])
                load_section(l, AT_PLE, KD, lambda n: w_ple[l - 1, n, :, :])
            for k in range(KD):
                sp.wait_ge(x_done, LAYERS * KD + k + 1)
                sp.dma_start(out[:, k * T:(k + 1) * T], tile(x, k)).then_inc(out_stored, 16)
            sp.wait_ge(out_stored, 16 * KD)

        @block.gpsimd
        def _(pool):
            pool.memset(ident[:, :], 0.0).then_inc(zeroed, 1)
            pool.memset(causal[:, :], 0.0).then_inc(zeroed, 1)
            pool.memset(ones2[:, :], 1.0).then_inc(consts_ready, 1)
            pool.memset(halves[:, :], 0.0).then_inc(zeroed, 1)
            pool.memset(eps[:, :], EPS).then_inc(consts_ready, 1)
            pool.memset(u_pad[:, 0:2], 0.0).then_inc(consts_ready, 1)
            pool.wait_ge(zeroed, 3)
            pool.wait_ge(consts_ready, 3)
            pool.memset(halves[0:QK, 0:1], 1.0).then_inc(consts_ready, 1)
            pool.wait_ge(consts_ready, 4)
            pool.memset(halves[QK:P, 1:2], 1.0).then_inc(consts_ready, 1)
            pool.wait_ge(consts_ready, 5)
            pool.affine_select(out=ident[:, :], in_=ident[:, :], compare_op=ALU.not_equal, fill=1.0,
                               base=0, pattern=[[-1, P]], channel_multiplier=1).then_inc(consts_ready, 1)
            pool.affine_select(out=causal[:, :], in_=causal[:, :], compare_op=ALU.is_ge, fill=-1e30,
                               base=0, pattern=[[-1, P]], channel_multiplier=1).then_inc(consts_ready, 1)
        CONSTS = 7

        @block.tensor
        def _(pe):
            def passes(to, k, slot, right_hi, right_lo, start, stop):
                hi, lo = w_hi[slot][:, k * P:(k + 1) * P], w_lo[slot][:, k * P:(k + 1) * P]
                pe.matmul(to, hi, right_lo, start=start, stop=False)
                pe.matmul(to, hi, right_hi, start=False, stop=False)
                return pe.matmul(to, lo, right_hi, start=False, stop=stop)

            def group(l, turn, j, right, blocks, tile_ready=None, hooks=()):
                n = l * CHUNKS + 4 * turn + j
                pe.wait_ge(lo_split, n + 1)
                pe.wait_ge(drained, n - 1)
                hooks = list(hooks)
                for k in range(blocks):
                    if tile_ready:
                        tile_ready(k)
                    ins = passes(acc[j % 2][:, :], k, j % 2, tile(right[0], k), tile(right[1], k),
                                 k == 0, k == blocks - 1)
                    if k == blocks - 1:
                        ins.then_inc(group_done, 1)
                    while hooks and hooks[0][0] <= k:
                        hooks.pop(0)[1]()

            def column_sums(nu, of, which, ready, count):
                pe.wait_ge(ready, count)
                pe.wait_ge(std_done, nu)
                for j in range(4):
                    ins = pe.matmul(sums[:, 2 * j:2 * j + 2], of[:, j * P:(j + 1) * P], which[:, :],
                                    start=True, stop=True)
                ins.then_inc(sums_done, 1)

            def spread_factors(nu):
                pe.wait_ge(wide_done, nu + 1)
                pe.wait_ge(norm_used, nu)
                for j in range(4):
                    ins = pe.matmul(spread[:, j * P:(j + 1) * P], inv_wide[:, j * P:(j + 1) * P], ident[:, :],
                                    start=True, stop=True)
                ins.then_inc(spread_done, 1)

            def resid_hooks(l, s):
                nu = l * NORMS + RESID_AT[s]
                return ([(KD - 1, lambda: column_sums(nu, square_sum, ones2, sq_x_added, (l * RESID + s + 1) * (KD - 1)))],
                        [(3, lambda: spread_factors(nu))])

            def h_ready(l, s):
                return lambda k: pe.wait_ge(h_lo_done, (l * RESID + s) * KD + k + 1)

            def section(l, turn, turns, right, blocks, ready=None, hooks=((), ())):
                if ready:
                    for j in range(4):
                        group(l, turn, j, right, blocks, tile_ready=ready if j == 0 else None,
                              hooks=hooks[j] if j < 2 else ())
                with pe.Fori(1 if ready else 0, turns) as i:
                    for j in range(4):
                        group(l, turn + i, j, right, blocks)

            def ffn(l, f):
                turn = AT_FFN[f] // 4
                for part, tiles in enumerate(PARTS):
                    if part == 0:
                        section(l, turn, tiles // 2, (h_hi, h_lo), KD, ready=h_ready(l, 2 * f),
                                hooks=resid_hooks(l, 2 * f))
                    else:
                        section(l, turn, tiles // 2, (h_hi, h_lo), KD)
                    turn += tiles // 2
                    section(l, turn, KD // 4, (a_hi, a_lo), tiles,
                            ready=lambda k: pe.wait_ge(a_lo_done, inner(l, f, part, k) + 1))
                    turn += KD // 4

            def mix_task(l, task, head):
                h, i = head if isinstance(head, tuple) else (head, 0)
                c = l * HEADS + h
                e = 4 * c + i
                s = h % 2
                if task.endswith("_sum"):
                    at = NORM_AT[task[0], h]
                    column_sums(l * NORMS + at, square, ones2 if task == "o_sum" else halves,
                                square_done, l * 4 * HEADS + at - 2 + 1)
                elif task.endswith("_spread"):
                    spread_factors(l * NORMS + NORM_AT[task[0], h])
                elif task == "v_turn":
                    pe.wait_ge(drained, l * CHUNKS + AT_MIX + MIX.index(("v", h)) + 1)
                    pe.wait_ge(o_ready, c)
                    for j in range(4):
                        ins = pe.transpose(values[:, j * P:(j + 1) * P], v_t[:, j * P:(j + 1) * P], ident[:, :])
                    ins.then_inc(v_turned, 1)
                elif task == "score":
                    pe.wait_ge(norm_used, l * NORMS + NORM_AT["k", h] + 1)
                    pe.wait_ge(exp_done, e)
                    n = P * (i + 1)
                    for m in range(2):
                        rows = slice(QK * m, QK * (m + 1))
                        ins = pe.matmul(scores[:, m * T:m * T + n], q_t[s][rows, i * P:(i + 1) * P],
                                        k_t[s][rows, 0:n], start=True, stop=True)
                    ins.then_inc(scores_done, 1)
                elif task == "turn":
                    pe.wait_ge(diff_ready, e + 1)
                    pe.wait_ge(diff_t_ready, e)
                    for j in range(i + 1):
                        at = diff_at[i] + j * P
                        ins = pe.transpose(turned[:, j * P:(j + 1) * P], diff[:, at:at + P], ident[:, :])
                    ins.then_inc(turn_done, 1)
                elif task == "attend":
                    pe.wait_ge(v_rows_ready, c + 1)
                    pe.wait_ge(diff_t_ready, 4 * c + 4)
                    for j in range(4):
                        ins = pe.matmul(values[:, j * P:T], v_rows[s][:, j * P:(j + 1) * P],
                                        diff_t[:, j * T + j * P:(j + 1) * T], start=j == 0, stop=j == 3)
                    ins.then_inc(attended, 1)

            def mixer_hooks(l, c):
                return [(k, lambda task=task, head=head: mix_task(l, task, head)) for k, task, head in HOOKS.get(c, [])]

            def mixer(l):
                resid = resid_hooks(l, 1)
                for c in range(len(MIX)):
                    group(l, (AT_MIX + c) // 4, c % 4, (h_hi, h_lo), KD,
                          tile_ready=h_ready(l, 1) if c == 0 else None,
                          hooks=resid[c] if c < 2 else mixer_hooks(l, c))

            def project(l):
                def y_ready(k):
                    pe.wait_ge(y_lo_done, l * 2 * HEADS + Y_AT[("o", k) if k < HEADS else ("c", k - HEADS)] + 1)
                section(l, AT_OUT // 4, KD // 4, (a_hi, a_lo), KD, ready=y_ready,
                        hooks=[mixer_hooks(l, len(MIX) + j) for j in range(2)])

            def embed(l):
                def both(turn, j, **how):
                    m = 4 * (turn - AT_PLE // 4) + j
                    pe.wait_ge(lo_split, l * CHUNKS + 4 * turn + j + 1)
                    pe.wait_ge(gated, l * KD + m - 1)
                    if isinstance(m, int) and m == 0:
                        pe.wait_ge(exp_done, (l + 1) * 4 * HEADS)
                        pe.wait_ge(p_lo_done, l + 1)
                    for k in range(KP):
                        passes(scores[:, (j % 2) * T:(j % 2 + 1) * T], KD + k, j % 2, tile(p_hi, k), tile(p_lo, k),
                               k == 0, k == KP - 1)
                    group(l, turn, j, (h_hi, h_lo), KD, **how)
                resid = resid_hooks(l, 3)
                for j in range(4):
                    both(AT_PLE // 4, j, tile_ready=h_ready(l, 3) if j == 0 else None, hooks=resid[j] if j < 2 else ())
                with pe.Fori(1, KD // 4) as i:
                    for j in range(4):
                        both(AT_PLE // 4 + i, j)

            pe.wait_ge(consts_ready, CONSTS)
            for semaphore, count in (
                (group_done, CHUNKS),
                (sums_done, NORMS),
                (spread_done, NORMS),
                (v_turned, HEADS),
                (scores_done, 4 * HEADS),
                (turn_done, 4 * HEADS),
                (attended, HEADS),
            ):
                pe.sem_inc(semaphore, count)
            with pe.Fori(1, LAYERS + 1) as l:
                ffn(l, 0)
                mixer(l)
                project(l)
                ffn(l, 1)
                embed(l)

        @block.scalar
        def _(act):
            def split(l, turn, j, blocks):
                w = blocks * P
                act.wait_ge(raw_loaded[j], 16 * (l * (CHUNKS // RAW) + turn + 1))
                act.activation(w_hi[j % 2][:, 0:w], raw[j][:, 0:w], ACT.Copy).then_inc(hi_split, 1)

            def result(l, turn, j):
                act.wait_ge(group_done, l * CHUNKS + 4 * turn + j + 1)

            def norm_tile(l, s, k, gain_at):
                if k == 0:
                    act.wait_ge(std_done, l * NORMS + RESID_AT[s])
                elif k > 1:
                    act.wait_ge(sq_x_added, (l * RESID + s) * (KD - 1) + k - 1)
                to = square_sum if k == 0 else square_x
                act.activation(to[:, :], tile(x, k), ACT.Square).then_inc(sq_x_done, 1)
                act.activation(tile(h_hi, k), tile(x, k), ACT.Copy,
                               scale=gain[:, gain_at + k:gain_at + k + 1]).then_inc(h_hi_done, 1)

            def take_std(nu, width):
                act.wait_ge(sums_done, nu + 1)
                act.wait_ge(inv_done, nu)
                act.activation(std[:, :], sums[:, 0:8], ACT.Sqrt, scale=1.0 / width,
                               bias=eps[:, 0:1]).then_inc(std_done, 1)

            def resid_norm(l, s):
                nu = l * NORMS + RESID_AT[s]
                take_std(nu, D)
                act.wait_ge(spread_done, nu + 1)
                act.activation(rstd[:, :], spread[:, :], ACT.Copy).then_inc(norm_used, 1)

            def ffn(l, f):
                turn = AT_FFN[f] // 4
                for part, tiles in enumerate(PARTS):
                    def two_tiles(i, blocks_next=KD, norm=False):
                        for half in range(2):
                            t = inner(l, f, part, 2 * i + half)
                            gate, up = 2 * half, 2 * half + 1
                            result(l, turn + i, gate)
                            split(l, *ahead(turn + i, gate), blocks_next if half else KD)
                            if norm and half == 0:
                                resid_norm(l, 2 * f)
                            act.wait_ge(drained, l * CHUNKS + 4 * (turn + i) + gate + 1)
                            act.wait_ge(inner_done, t)
                            act.activation(tmp_b[:, :], tmp_a[:, :], ACT.Silu).then_inc(silu_done, 1)
                            result(l, turn + i, up)
                            split(l, *ahead(turn + i, up), blocks_next if half else KD)
                            act.wait_ge(inner_done, t + 1)
                            act.activation(dyn(a_hi, 2 * i + half), tmp_d[:, :], ACT.Copy).then_inc(a_hi_done, 1)

                    if part == 0:
                        two_tiles(0, norm=True)
                    with act.Fori(1 if part == 0 else 0, tiles // 2 - 1) as i:
                        two_tiles(i)
                    two_tiles(tiles // 2 - 1, blocks_next=tiles)
                    turn += tiles // 2
                    after = KD if part == 0 or f == 0 else PLE_BLOCKS
                    for m in range(KD):
                        at, j = turn + m // 4, m % 4
                        result(l, at, j)
                        split(l, *ahead(at, j), tiles if m < KD - 2 else after)
                        if part == 1:
                            act.wait_ge(drained, l * CHUNKS + 4 * at + j + 1)
                            norm_tile(l, 2 * f + 1, m, G_MIX if f == 0 else G_PLE)
                    turn += KD // 4

            def take_square(l, kind, h, of):
                act.wait_ge(sums_done, l * NORMS + NORM_AT[kind, h])
                act.activation(square[:, :], of[:, :], ACT.Square).then_inc(square_done, 1)

            def mix_task(l, task, head):
                h, i = head if isinstance(head, tuple) else (head, 0)
                c = l * HEADS + h
                e = 4 * c + i
                s = h % 2
                if task.endswith("_sum"):
                    take_std(l * NORMS + NORM_AT[task[0], h], P if task == "o_sum" else QK)
                elif task in ("o_spread", "c_spread"):
                    act.wait_ge(norm_used, l * NORMS + NORM_AT[task[0], h] + 1)
                    act.activation(tile(a_hi, h + (HEADS if task == "c_spread" else 0)), tmp_d[:, :],
                                   ACT.Copy).then_inc(y_hi_done, 1)
                elif task == "v_turn":
                    act.wait_ge(v_turned, c + 1)
                    act.activation(v_rows[s][:, :], values[:, :], ACT.Copy).then_inc(v_rows_ready, 1)
                elif task == "score":
                    n = P * (i + 1)
                    act.wait_ge(max_ready, e + 1)
                    act.wait_ge(diff_ready, e)
                    if (h, i) == (0, 0):
                        act.wait_ge(p_lo_done, l + 1)
                    for m in range(2):
                        ins = act.activation(exps[:, m * T:m * T + n], scores[:, m * T:m * T + n], ACT.Exp,
                                             scale=QK ** -0.5, bias=row_max[:, m:m + 1],
                                             accum_out=row_sum[:, m:m + 1])
                    ins.then_inc(exp_done, 1)
                elif task == "turn":
                    act.wait_ge(turn_done, e + 1)
                    act.wait_ge(attended, c)
                    act.activation(diff_t[:, :].rearrange("p (j q) -> p j q", q=T)[:, 0:i + 1, i * P:(i + 1) * P],
                                   turned[:, 0:(i + 1) * P].rearrange("p (j q) -> p j q", q=P),
                                   ACT.Copy).then_inc(diff_t_ready, 1)
                elif task == "attend":
                    act.wait_ge(attended, c + 1)
                    if h:
                        act.wait_ge(norm_used, l * NORMS + NORM_AT["o", h - 1] + 1)
                    act.activation(o_t[:, :], values[:, :], ACT.Copy).then_inc(o_ready, 1)
                    act.wait_ge(o_ready, c + 1)
                    take_square(l, "o", h, o_t)

            def mixer(l):
                for c, (kind, h) in enumerate(MIX):
                    turn, j = (AT_MIX + c) // 4, c % 4
                    result(l, turn, j)
                    split(l, *ahead(turn, j), KD)
                    if c == 0:
                        resid_norm(l, 1)
                    if kind in "qk":
                        act.wait_ge(drained, l * CHUNKS + AT_MIX + c + 1)
                        take_square(l, kind, h, (q_t if kind == "q" else k_t)[h % 2])
                    if kind == "b":
                        act.wait_ge(conv_done, l * HEADS + h + 1)
                        take_square(l, "c", h, tmp_c)
                    for _, task, head in HOOKS.get(c + 1, []):
                        mix_task(l, task, head)

            def project(l):
                for m in range(KD):
                    turn, j = (AT_OUT + m) // 4, m % 4
                    result(l, turn, j)
                    split(l, *ahead(turn, j), KD)
                    for _, task, head in HOOKS.get(len(MIX) + m + 1, []):
                        mix_task(l, task, head)
                    act.wait_ge(drained, l * CHUNKS + AT_OUT + m + 1)
                    norm_tile(l, 2, m, G_FFN2)

            def embed(l):
                for m in range(KD):
                    turn, j = (AT_PLE + m) // 4, m % 4
                    result(l, turn, j)
                    if m < KD - 2:
                        split(l, *ahead(turn, j), PLE_BLOCKS)
                    if m == 0:
                        resid_norm(l, 3)
                    act.wait_ge(drained, l * CHUNKS + AT_PLE + m + 1)
                    act.wait_ge(gated, l * KD + m)
                    act.activation(tmp_b[:, :], tmp_a[:, :], ACT.Sigmoid).then_inc(sigmoid_done, 1)

            act.wait_ge(setup_step, 2)
            act.activation(lam_exp[:, :], lam_sum[:, :], ACT.Exp).then_inc(lam_exp_ready, 1)
            act.wait_ge(consts_ready, CONSTS)
            act.wait_ge(x_loaded, 16 * KD)
            for semaphore, count in (
                (hi_split, CHUNKS),
                (h_hi_done, RESID * KD),
                (sq_x_done, RESID * KD),
                (square_done, 4 * HEADS),
                (std_done, NORMS),
                (norm_used, RESID),
                (silu_done, 2 * sum(PARTS)),
                (a_hi_done, 2 * sum(PARTS)),
                (v_rows_ready, HEADS),
                (exp_done, 4 * HEADS),
                (diff_t_ready, 4 * HEADS),
                (o_ready, HEADS),
                (y_hi_done, 2 * HEADS),
                (p_hi_done, 1),
                (sigmoid_done, KD),
            ):
                act.sem_inc(semaphore, count)
            with act.Fori(1, LAYERS + 1) as l:
                act.wait_ge(gain_ready, 2 * l + 2)
                act.wait_ge(group_done, l * CHUNKS)
                for j in range(2):
                    split(l, 0, j, KD)
                for k in range(KD):
                    act.wait_ge(x_done, l * KD)
                    norm_tile(l, 0, k, G_FFN1)
                act.wait_ge(p_loaded, 16 * l + 16)
                act.activation(p_hi[:, :], p_raw[:, :], ACT.Copy).then_inc(p_hi_done, 1)
                ffn(l, 0)
                mixer(l)
                project(l)
                ffn(l, 1)
                embed(l)

        @block.vector
        def _(dve):
            def split(l, turn, j, blocks):
                w = blocks * P
                dve.wait_ge(hi_split, l * CHUNKS + 4 * turn + j + 1)
                dve.wait_ge(raw_loaded[j], 16 * (l * (CHUNKS // RAW) + turn + 1))
                dve.tensor_tensor(w_lo[j % 2][:, 0:w], raw[j][:, 0:w],
                                  w_hi[j % 2][:, 0:w].bitcast(f32), ALU.subtract).then_inc(lo_split, 1)

            def result(l, turn, j):
                dve.wait_ge(group_done, l * CHUNKS + 4 * turn + j + 1)

            def scaled(l, turn, j, to):
                dve.tensor_tensor(to, acc[j % 2][:, :], rstd[:, :], ALU.mult).then_inc(drained, 1)
                return l * CHUNKS + 4 * turn + j + 1

            def into_x(l, turn, j, m, factor):
                dve.scalar_tensor_tensor(out=tile(x, m), in0=acc[j % 2][:, :], scalar=factor, in1=tile(x, m),
                                         op0=ALU.mult, op1=ALU.add).then_inc(drained, 1)

            def norm_tile(l, s, k, gain_at):
                t, added = (l * RESID + s) * KD + k, (l * RESID + s) * (KD - 1) + k - 1
                if k:
                    dve.wait_ge(sq_x_done, t + 1)
                    if k > 1:
                        dve.wait_ge(sq_x_added, added)
                    dve.tensor_tensor(square_sum[:, :], square_sum[:, :], square_x[:, :],
                                      ALU.add).then_inc(sq_x_added, 1)
                dve.wait_ge(h_hi_done, t + 1)
                dve.scalar_tensor_tensor(out=tile(h_lo, k), in0=tile(x, k),
                                         scalar=gain[:, gain_at + k:gain_at + k + 1],
                                         in1=tile(h_hi, k).bitcast(f32), op0=ALU.mult,
                                         op1=ALU.subtract).then_inc(h_lo_done, 1)

            def take_inv(nu):
                dve.wait_ge(std_done, nu + 1)
                dve.reciprocal(inv[:, :], std[:, :]).then_inc(inv_done, 1)
                dve.wait_ge(inv_done, nu + 1)
                dve.wait_ge(spread_done, nu)
                dve.tensor_copy(inv_wide[:, :].rearrange("p (c d) -> p c d", d=QK),
                                inv[:, :].unsqueeze(2).broadcast_to([P, 8, QK])).then_inc(wide_done, 1)

            def resid_norm(l, s):
                take_inv(l * NORMS + RESID_AT[s])
                dve.wait_ge(norm_used, l * NORMS + RESID_AT[s] + 1)

            def ffn(l, f):
                turn = AT_FFN[f] // 4
                for part, tiles in enumerate(PARTS):
                    def two_tiles(i, blocks_next=KD, norm=False):
                        for half in range(2):
                            t = inner(l, f, part, 2 * i + half)
                            gate, up = 2 * half, 2 * half + 1
                            result(l, turn + i, gate)
                            split(l, *ahead(turn + i, gate), blocks_next if half else KD)
                            if norm and half == 0:
                                resid_norm(l, 2 * f)
                            dve.wait_ge(silu_done, t)
                            scaled(l, turn + i, gate, tmp_a[:, :])
                            result(l, turn + i, up)
                            split(l, *ahead(turn + i, up), blocks_next if half else KD)
                            count = scaled(l, turn + i, up, tmp_c[:, :])
                            dve.wait_ge(drained, count)
                            dve.wait_ge(silu_done, t + 1)
                            dve.wait_ge(a_hi_done, t)
                            dve.tensor_tensor(tmp_d[:, :], tmp_b[:, :], tmp_c[:, :], ALU.mult).then_inc(inner_done, 1)
                            dve.wait_ge(inner_done, t + 1)
                            dve.wait_ge(a_hi_done, t + 1)
                            dve.tensor_tensor(dyn(a_lo, 2 * i + half), tmp_d[:, :],
                                              dyn(a_hi, 2 * i + half).bitcast(f32), ALU.subtract).then_inc(a_lo_done, 1)

                    if part == 0:
                        two_tiles(0, norm=True)
                    with dve.Fori(1 if part == 0 else 0, tiles // 2 - 1) as i:
                        two_tiles(i)
                    two_tiles(tiles // 2 - 1, blocks_next=tiles)
                    turn += tiles // 2
                    after = KD if part == 0 or f == 0 else PLE_BLOCKS
                    for m in range(KD):
                        at, j = turn + m // 4, m % 4
                        result(l, at, j)
                        split(l, *ahead(at, j), tiles if m < KD - 2 else after)
                        into_x(l, at, j, m, 0.5)
                        if part == 1:
                            dve.wait_ge(drained, l * CHUNKS + 4 * at + j + 1)
                            norm_tile(l, 2 * f + 1, m, G_MIX if f == 0 else G_PLE)
                    turn += KD // 4

            def link(l, h, step, ins):
                ins.then_inc(conv_step, 1)
                dve.wait_ge(conv_step, (l * HEADS + h) * CONV_STEPS + step + 1)

            def convolve(l, h):
                taps = [gain[:, G_CW + 4 * t + h:G_CW + 4 * t + h + 1] for t in range(3)]
                link(l, h, 0, dve.tensor_tensor(u_pad[:, 2:T + 2], tmp_a[:, :], tmp_b[:, :], ALU.mult))
                link(l, h, 1, dve.tensor_scalar(tmp_c[:, :], u_pad[:, 2:T + 2], taps[2],
                                                gain[:, G_CB + h:G_CB + h + 1], ALU.mult, ALU.add))
                for t in (1, 0):
                    link(l, h, 3 - t, dve.scalar_tensor_tensor(out=tmp_c[:, :], in0=u_pad[:, t:T + t], scalar=taps[t],
                                                               in1=tmp_c[:, :], op0=ALU.mult, op1=ALU.add))

            def norm_out(l, kind, h, of, gain_at):
                y = l * 2 * HEADS + Y_AT[kind, h]
                k = h + (HEADS if kind == "c" else 0)
                nu = l * NORMS + NORM_AT[kind, h]
                dve.wait_ge(spread_done, nu + 1)
                dve.wait_ge(y_hi_done, y)
                if kind == "o":
                    dve.wait_ge(o_ready, l * HEADS + h + 1)
                else:
                    dve.wait_ge(conv_done, l * HEADS + h + 1)
                dve.scalar_tensor_tensor(out=tmp_d[:, :], in0=of[:, :], scalar=gain_at, in1=spread[:, :],
                                         op0=ALU.mult, op1=ALU.mult).then_inc(norm_used, 1)
                dve.wait_ge(norm_used, nu + 1)
                dve.wait_ge(y_hi_done, y + 1)
                dve.tensor_tensor(tile(a_lo, k), tmp_d[:, :], tile(a_hi, k).bitcast(f32),
                                  ALU.subtract).then_inc(y_lo_done, 1)

            def softmax(l, h, i):
                e = 4 * (l * HEADS + h) + i
                n = P * (i + 1)
                both = scores[:, :].rearrange("p (m k) -> p m k", m=2)
                dve.wait_ge(scores_done, e + 1)
                dve.wait_ge(exp_done, e)
                dve.tensor_tensor(both[:, :, i * P:n], both[:, :, i * P:n],
                                  causal[:, :].unsqueeze(1).broadcast_to([P, 2, P]), ALU.add).then_inc(masked, 1)
                dve.wait_ge(masked, e + 1)
                dve.tensor_reduce(row_top[:, :], both[:, :, 0:n], AX.X, ALU.max).then_inc(max_done, 1)
                dve.wait_ge(max_done, e + 1)
                dve.tensor_scalar(row_max[:, :], row_top[:, :], -(QK ** -0.5), None, ALU.mult).then_inc(max_ready, 1)
                dve.wait_ge(exp_done, e + 1)
                dve.reciprocal(row_inv[:, :], row_sum[:, :]).then_inc(inv_step, 1)
                dve.wait_ge(inv_step, 2 * e + 1)
                dve.tensor_tensor(row_inv[:, 1:2], row_inv[:, 1:2], neg_lam_now[:, :], ALU.mult).then_inc(inv_step, 1)
                dve.wait_ge(inv_step, 2 * e + 2)
                dve.wait_ge(turn_done, e - 3)
                to = diff[:, diff_at[i]:diff_at[i] + n]
                dve.tensor_scalar(to, exps[:, 0:n], row_inv[:, 0:1], None, ALU.mult).then_inc(diff_step, 1)
                dve.wait_ge(diff_step, e + 1)
                dve.scalar_tensor_tensor(out=to, in0=exps[:, T:T + n], scalar=row_inv[:, 1:2], in1=to,
                                         op0=ALU.mult, op1=ALU.add).then_inc(diff_ready, 1)

            def mix_task(l, task, head):
                h, i = head if isinstance(head, tuple) else (head, 0)
                if task.endswith("_sum"):
                    take_inv(l * NORMS + NORM_AT[task[0], h])
                elif task in ("q_spread", "k_spread"):
                    of, g = (q_t[h % 2], G_Q) if task == "q_spread" else (k_t[h % 2], G_K)
                    dve.wait_ge(spread_done, l * NORMS + NORM_AT[task[0], h] + 1)
                    dve.scalar_tensor_tensor(out=of[:, :], in0=of[:, :], scalar=gain[:, g:g + 1],
                                             in1=spread[:, :], op0=ALU.mult, op1=ALU.mult).then_inc(norm_used, 1)
                elif task == "o_spread":
                    norm_out(l, "o", h, o_t, gain[:, G_O:G_O + 1])
                elif task == "c_spread":
                    norm_out(l, "c", h, tmp_c, gain[:, G_CN + h:G_CN + h + 1])
                elif task == "score":
                    softmax(l, h, i)

            def mixer(l):
                for c, (kind, h) in enumerate(MIX):
                    turn, j = (AT_MIX + c) // 4, c % 4
                    result(l, turn, j)
                    split(l, *ahead(turn, j), KD)
                    if c == 0:
                        resid_norm(l, 1)
                    if kind in "qk":
                        dve.wait_ge(scores_done, 4 * (l * HEADS + h - 1))
                    if kind == "v":
                        dve.wait_ge(v_turned, l * HEADS + h)
                    to = {"q": q_t[h % 2], "k": k_t[h % 2], "v": v_t, "c": tmp_a, "h": tmp_b, "b": tmp_b}[kind]
                    count = scaled(l, turn, j, to[:, :])
                    if kind == "h":
                        dve.wait_ge(drained, count)
                        convolve(l, h)
                    if kind == "b":
                        dve.wait_ge(drained, count)
                        dve.tensor_tensor(tmp_c[:, :], tmp_c[:, :], tmp_b[:, :], ALU.mult).then_inc(conv_done, 1)
                    for _, task, head in HOOKS.get(c + 1, []):
                        mix_task(l, task, head)

            def project(l):
                for m in range(KD):
                    turn, j = (AT_OUT + m) // 4, m % 4
                    result(l, turn, j)
                    split(l, *ahead(turn, j), KD)
                    for _, task, head in HOOKS.get(len(MIX) + m + 1, []):
                        mix_task(l, task, head)
                    into_x(l, turn, j, m, 1.0)
                    dve.wait_ge(drained, l * CHUNKS + AT_OUT + m + 1)
                    norm_tile(l, 2, m, G_FFN2)

            def embed(l):
                for m in range(KD):
                    turn, j = (AT_PLE + m) // 4, m % 4
                    result(l, turn, j)
                    if m < KD - 2:
                        split(l, *ahead(turn, j), PLE_BLOCKS)
                    if m == 0:
                        resid_norm(l, 3)
                    dve.wait_ge(sigmoid_done, l * KD + m)
                    scaled(l, turn, j, tmp_a[:, :])
                    dve.wait_ge(sigmoid_done, l * KD + m + 1)
                    dve.tensor_tensor(tmp_c[:, :], scores[:, (j % 2) * T:(j % 2 + 1) * T], tmp_b[:, :],
                                      ALU.mult).then_inc(gated, 1)
                    dve.wait_ge(gated, l * KD + m + 1)
                    dve.tensor_tensor(tile(x, m), tile(x, m), tmp_c[:, :], ALU.add).then_inc(x_done, 1)

            dve.wait_ge(consts_loaded, 32)
            pairs = lam_vecs[:, :].rearrange("p (m a d) -> p m a d", a=2, d=QK)
            products = lam_prod[:, :].rearrange("p (m d) -> p m d", d=QK)
            dve.tensor_tensor(products, pairs[:, :, 0, :], pairs[:, :, 1, :], ALU.mult).then_inc(setup_step, 1)
            dve.wait_ge(setup_step, 1)
            dve.tensor_reduce(lam_sum[:, :], products, AX.X, ALU.add).then_inc(setup_step, 1)
            dve.wait_ge(lam_exp_ready, 1)
            for l in range(LAYERS):
                lam, g = neg_lam[:, l:l + 1], vecs[:, l * GAINS + G_O:l * GAINS + G_O + 1]
                dve.tensor_tensor(lam, lam_exp[:, 2 * l + 1:2 * l + 2], lam_exp[:, 2 * l:2 * l + 1],
                                  ALU.subtract).then_inc(setup_step, 1)
                dve.wait_ge(setup_step, 3 + 2 * l)
                dve.tensor_scalar(lam, lam, -lambda_init(l), None, ALU.add).then_inc(setup_step, 1)
                dve.tensor_scalar(g, g, 1.0 - lambda_init(l), None, ALU.mult).then_inc(gain_scaled, 1)
            dve.wait_ge(setup_step, 2 + 2 * LAYERS)
            dve.wait_ge(gain_scaled, LAYERS)
            dve.wait_ge(consts_ready, CONSTS)
            dve.wait_ge(x_loaded, 16 * KD)
            for semaphore, count in (
                (lo_split, CHUNKS),
                (drained, CHUNKS),
                (x_done, KD),
                (h_lo_done, RESID * KD),
                (sq_x_added, RESID * (KD - 1)),
                (inv_done, NORMS),
                (wide_done, NORMS),
                (norm_used, NORMS - RESID),
                (inner_done, 2 * sum(PARTS)),
                (a_lo_done, 2 * sum(PARTS)),
                (masked, 4 * HEADS),
                (max_done, 4 * HEADS),
                (max_ready, 4 * HEADS),
                (inv_step, 8 * HEADS),
                (diff_step, 4 * HEADS),
                (diff_ready, 4 * HEADS),
                (conv_step, HEADS * CONV_STEPS),
                (conv_done, HEADS),
                (y_lo_done, 2 * HEADS),
                (p_lo_done, 1),
                (gated, KD),
                (gain_ready, 2),
            ):
                dve.sem_inc(semaphore, count)
            with dve.Fori(1, LAYERS + 1) as l:
                dve.wait_ge(h_hi_done, l * RESID * KD)
                dve.tensor_copy(gain[:, :], vecs[:, bass.ds((l - 1) * GAINS, GAINS)]).then_inc(gain_ready, 1)
                dve.tensor_copy(neg_lam_now[:, :], neg_lam[:, bass.ds(l - 1, 1)]).then_inc(gain_ready, 1)
                dve.wait_ge(gain_ready, 2 * l + 2)
                dve.wait_ge(x_done, l * KD)
                dve.wait_ge(group_done, l * CHUNKS)
                for j in range(2):
                    split(l, 0, j, KD)
                for k in range(KD):
                    norm_tile(l, 0, k, G_FFN1)
                dve.wait_ge(p_hi_done, l + 1)
                dve.tensor_tensor(p_lo[:, :], p_raw[:, :], p_hi[:, :].bitcast(f32), ALU.subtract).then_inc(p_lo_done, 1)
                ffn(l, 0)
                mixer(l)
                project(l)
                ffn(l, 1)
                embed(l)


def blocked(w, tiles_in):
    lead = w.shape[:-2]
    w = w.reshape(*lead, tiles_in, P, w.shape[-1] // P, P)
    n = len(lead)
    w = w.transpose(*range(n), n + 2, n + 1, n, n + 3)
    return np.ascontiguousarray(w.reshape(*lead, w.shape[n], P, tiles_in * P))


def columns(v):
    return v.reshape(LAYERS, -1, P).transpose(0, 2, 1)


def kernel(**inputs):
    import concourse.bacc as bacc
    from concourse.bass_utils import run_bass_kernel_spmd as run

    a = {name: np.asarray(v) for name, v in inputs.items()}
    arrays = {}
    gate_up = []
    for f in ("ffn1", "ffn2"):
        g, u = (blocked(a[f"{f}_w_{s}"], KD) for s in ("gate", "up"))
        gate_up.append(np.stack([g, u], axis=2).reshape(LAYERS, -1, P, KD * P))
    arrays["w_gu"] = np.stack(gate_up, axis=1)
    row = 0
    for part, tiles in enumerate(PARTS):
        arrays[f"w_down{part}"] = np.stack(
            [blocked(a[f"{f}_w_down"][:, row:row + tiles * P], tiles) for f in ("ffn1", "ffn2")], axis=1)
        row += tiles * P
    w_in = blocked(a["w_in"], KD)
    arrays["w_mix"] = np.stack([w_in[:, COLUMN[kind] + h] for kind, h in MIX], axis=1)
    arrays["w_out"] = blocked(a["w_out"], KD)
    arrays["w_ple"] = np.concatenate([blocked(a["ple_w_gate"], KD), blocked(a["ple_w_proj"], KP)], axis=-1)
    arrays["x_in"] = a["x"].reshape(T, KD, P).transpose(2, 1, 0).reshape(P, KD * T)
    arrays["p_in"] = a["p"].reshape(LAYERS, T, KP, P).transpose(0, 3, 2, 1).reshape(LAYERS, P, KP * T)
    vec = [columns(a[n]) for n in ("ffn1_norm", "mix_norm", "ffn2_norm", "ple_norm")]
    vec += [columns(np.tile(a[n], (1, 2))) for n in ("q_norm", "k_norm")]
    vec += [columns(a[n]) for n in ("attn_out_norm", "conv_b", "conv_out_norm")]
    vec.append(columns(a["conv_w"]))
    vec = np.concatenate(vec, axis=2)
    arrays["vec_in"] = vec.transpose(1, 0, 2).reshape(P, LAYERS * GAINS)
    arrays["lam_in"] = np.stack([a[f"lambda_{s}"] for s in ("q1", "k1", "q2", "k2")], axis=1).reshape(-1)
    arrays = {name: np.ascontiguousarray(v) for name, v in arrays.items()}

    nc = bacc.Bacc("TRN2", target_bir_lowering=False, num_devices=1)
    dram = {name: nc.dram_tensor(name, v.shape, mybir.dt.from_np(v.dtype), kind="ExternalInput").ap()
            for name, v in arrays.items()}
    out = nc.dram_tensor("out", (P, KD * T), mybir.dt.float32, kind="ExternalOutput").ap()
    downs = [dram.pop(f"w_down{part}") for part in range(len(PARTS))]
    build(nc, w_down=downs, out=out, **dram)
    got = run(nc, [arrays], core_ids=[0]).results[0]["out"]
    return np.ascontiguousarray(got.reshape(P, KD, T).transpose(2, 1, 0)).reshape(1, T, D)
```

```python
from contextlib import ExitStack
import math

import numpy as np
import concourse.bass as bass
from concourse import mybir

P = 128
T = 512
D = 1024
KD = D // P
D_FF = 2816
LAYERS = 2
D_PLE = 256
KP = D_PLE // P
HEADS = 4
QK = 64
EPS = 1e-6
PARTS = (8, 8, 6)
assert sum(PARTS) * P == D_FF
assert max(PARTS) <= KD
PLE_BLOCKS = KD + KP

MIX = ([(k, 0) for k in "qkv"] + [(k, 1) for k in "qkv"] + [(k, 0) for k in "chb"]
       + [(k, 2) for k in "qkv"] + [(k, 1) for k in "chb"] + [(k, 3) for k in "qkv"]
       + [(k, 2) for k in "chb"] + [(k, 3) for k in "chb"])
COLUMN = {"q": 0, "k": 4, "v": 8, "b": 12, "c": 16, "h": 20}

FFN_CHUNKS = sum(2 * f + KD for f in PARTS)
AT_FFN = (0, FFN_CHUNKS + len(MIX) + KD)
AT_MIX = FFN_CHUNKS
AT_OUT = AT_MIX + len(MIX)
AT_PLE = AT_FFN[1] + FFN_CHUNKS
CHUNKS = AT_PLE + KD
SLOTS = 4
BLOCKS = PLE_BLOCKS
assert BLOCKS >= max(PARTS)

G_FFN1, G_MIX, G_FFN2, G_PLE = (KD * s for s in range(4))
G_Q = 4 * KD
G_K = G_Q + 1
G_O = G_K + 1
G_CB = G_O + 1
G_CN = G_CB + 4
G_CW = G_CN + 4
GAINS = G_CW + 12

RESID = 4
NORMS = RESID + 4 * HEADS


def lambda_init(layer):
    return 0.8 - 0.6 * math.exp(-0.3 * layer)


HOOKS = {
    2: [(3, "q_sum", 0), (6, "k_sum", 0), (7, "q_spread", 0)],
    3: [(2, "k_spread", 0), (6, "score", (0, 0)), (7, "weigh", (0, 0))],
    4: [(1, "score", (0, 1)), (7, "q_sum", 1)],
    5: [(0, "turn", (0, 0)), (1, "weigh", (0, 1)), (1, "v_turn", 0), (4, "score", (0, 2)), (4, "q_spread", 1),
        (7, "turn", (0, 1))],
    6: [(0, "k_sum", 1), (1, "score", (0, 3)), (3, "k_spread", 1), (4, "weigh", (0, 2))],
    7: [(0, "turn", (0, 2)), (0, "weigh", (0, 3)), (6, "score", (1, 0)), (7, "turn", (0, 3))],
    8: [(1, "weigh", (1, 0)), (3, "attend", 0), (3, "score", (1, 1)), (6, "o_sum", 0)],
    9: [(1, "o_spread", 0), (1, "weigh", (1, 1)), (4, "turn", (1, 0)), (4, "v_turn", 1), (6, "c_sum", 0),
        (6, "score", (1, 2))],
    10: [(0, "weigh", (1, 2)), (1, "turn", (1, 1)), (3, "score", (1, 3)), (4, "c_spread", 0), (6, "q_sum", 2)],
    11: [(0, "weigh", (1, 3)), (4, "turn", (1, 2)), (4, "k_sum", 2), (6, "turn", (1, 3)), (6, "q_spread", 2)],
    12: [(3, "attend", 1), (3, "k_spread", 2), (5, "o_sum", 1), (6, "score", (2, 0))],
    13: [(0, "weigh", (2, 0)), (1, "o_spread", 1), (5, "score", (2, 1))],
    14: [(1, "turn", (2, 0)), (1, "weigh", (2, 1)), (1, "v_turn", 2), (5, "score", (2, 2))],
    15: [(1, "weigh", (2, 2)), (2, "turn", (2, 1)), (2, "score", (2, 3))],
    16: [(1, "c_sum", 1), (1, "turn", (2, 2)), (1, "weigh", (2, 3)), (6, "q_sum", 3), (7, "turn", (2, 3))],
    17: [(0, "c_spread", 1), (4, "attend", 2), (4, "q_spread", 3), (4, "k_sum", 3)],
    18: [(0, "o_sum", 2), (1, "k_spread", 3), (4, "o_spread", 2), (6, "score", (3, 0))],
    19: [(5, "score", (3, 1)), (7, "weigh", (3, 0)), (7, "v_turn", 3)],
    20: [(3, "weigh", (3, 1)), (4, "turn", (3, 0)), (4, "score", (3, 2))],
    21: [(0, "weigh", (3, 2)), (1, "turn", (3, 1)), (4, "score", (3, 3))],
    22: [(1, "c_sum", 2), (1, "weigh", (3, 3)), (2, "turn", (3, 2)), (7, "c_spread", 2), (7, "turn", (3, 3))],
    23: [(4, "attend", 3), (6, "o_sum", 3)],
    24: [(3, "o_spread", 3), (5, "c_sum", 3)],
    25: [(2, "c_spread", 3)],
}
SPLIT_BEFORE = (0, 0, 3, 4, 0, 0, 1, 0, 6, 2, 7, 0, 1, 2, 0, 4, 7, 4, 0, 0, 7, 6, 0, 0)
assert len(SPLIT_BEFORE) == len(MIX)
_ORDER = [(t[0], h) for c in sorted(HOOKS) for _, t, h in HOOKS[c] if t.endswith("_sum")]
_SPREADS = [(t[0], h) for c in sorted(HOOKS) for _, t, h in HOOKS[c] if t.endswith("_spread")]
assert _ORDER == _SPREADS and len(_ORDER) == 4 * HEADS
NORM_AT = {name: 2 + i for i, name in enumerate(_ORDER)}
RESID_AT = (0, 1, NORMS - 2, NORMS - 1)
Y_AT = {name: i for i, name in enumerate(n for n in _ORDER if n[0] in "oc")}
CONV_STEPS = 4


def build(nc, w_gu, w_down, w_mix, w_out, w_ple, x_in, p_in, vec_in, lam_in, out):
    f32, f32r = mybir.dt.float32, mybir.dt.float32r
    ALU, ACT, AX = mybir.AluOpType, mybir.ActivationFunctionType, mybir.AxisListType

    ctx = ExitStack()
    with ctx:
        def sb(name, cols, dt=f32):
            return ctx.enter_context(nc.sbuf_tensor(name, [P, cols], dt))

        def bank(name, banks=1):
            return ctx.enter_context(nc.psum_tensor(name, [P, banks * T], f32))

        def sem(name):
            return ctx.enter_context(nc.semaphore(name))

        x = sb("x", KD * T)
        h_hi, h_lo = sb("h_hi", KD * T, f32r), sb("h_lo", KD * T, f32r)
        a_hi, a_lo = sb("a_hi", KD * T, f32r), sb("a_lo", KD * T, f32r)
        raw = [sb(f"raw{s}", BLOCKS * P) for s in range(SLOTS)]
        w_hi = [sb(f"w_hi{s}", BLOCKS * P, f32r) for s in range(SLOTS)]
        w_lo = [sb(f"w_lo{s}", BLOCKS * P, f32r) for s in range(SLOTS)]
        p_hi, p_lo = sb("p_hi", KP * T, f32r), sb("p_lo", KP * T, f32r)
        rstd = sb("rstd", T)
        square_sum = sb("square_sum", T)
        square = sb("square", T)
        std, inv = sb("std", 8), sb("inv", 8)
        inv_wide = sb("inv_wide", T)
        tmp_a, tmp_b, tmp_c, tmp_d = (sb(f"tmp_{c}", T) for c in "abcd")
        q_t = [sb(f"q_t{s}", T) for s in range(2)]
        k_t = [sb(f"k_t{s}", T) for s in range(2)]
        v_t = sb("v_t", T)
        v_rows = [sb(f"v_rows{s}", T) for s in range(2)]
        exps = sb("exps", 2 * T)
        diff_at = [0, P, 3 * P, 6 * P]
        diff = sb("diff", 10 * P)
        diff_t = sb("diff_t", 4 * T)
        square_x = [square, diff_t[:, 0:T]]
        o_t = sb("o_t", T)
        u_pad = sb("u_pad", T + 2)
        row_top, row_max, row_sum, row_inv = (sb(f"row_{s}", 2) for s in ("top", "max", "sum", "inv"))
        ident, causal = sb("ident", P), sb("causal", P)
        ones2, halves = sb("ones2", 2), sb("halves", 2)
        eps = sb("eps", 1)
        vecs, gain = sb("vecs", LAYERS * GAINS), sb("gain", GAINS)
        lam_vecs = diff[:, 0:LAYERS * 4 * QK]
        lam_prod = o_t[:, 0:LAYERS * 2 * QK]
        lam_sum, lam_exp = sb("lam_sum", LAYERS * 2), sb("lam_exp", LAYERS * 2)
        neg_lam, neg_lam_now = sb("neg_lam", LAYERS), sb("neg_lam_now", 1)
        p_raw = exps

        acc = [bank(f"acc{s}") for s in range(2)]
        scores = bank("scores", 2)
        turned = bank("turned")
        values = bank("values")
        sums = bank("sums")
        spread = bank("spread")

        raw_loaded = [sem(f"raw_loaded{s}") for s in range(SLOTS)]
        x_loaded = [sem(f"x_loaded{k}") for k in range(KD)]
        consts_loaded, p_loaded, out_stored = (sem(s) for s in ("consts_loaded", "p_loaded", "out_stored"))
        zeroed, consts_ready, setup_step, lam_exp_ready, gain_scaled, gain_ready = (
            sem(s) for s in ("zeroed", "consts_ready", "setup_step", "lam_exp_ready", "gain_scaled", "gain_ready"))
        hi_split = sem("hi_split")
        lo_split = sem("lo_split")
        group_done = sem("group_done")
        drained = sem("drained")
        x_done = sem("x_done")
        h_hi_done, h_lo_done = sem("h_hi_done"), sem("h_lo_done")
        sq_x_done, sq_x_added = sem("sq_x_done"), sem("sq_x_added")
        square_done, sums_done, std_done, inv_done, wide_done, spread_done, norm_used = (
            sem(s) for s in ("square_done", "sums_done", "std_done", "inv_done", "wide_done", "spread_done", "norm_used"))
        silu_done, inner_done, a_hi_done, a_lo_done = (
            sem(s) for s in ("silu_done", "inner_done", "a_hi_done", "a_lo_done"))
        v_turned, v_rows_ready = sem("v_turned"), sem("v_rows_ready")
        scores_done, masked, max_done, max_ready, exp_done, inv_step, diff_step, diff_ready = (
            sem(s) for s in ("scores_done", "masked", "max_done", "max_ready", "exp_done", "inv_step", "diff_step", "diff_ready"))
        turn_done, diff_t_ready, attended, o_ready = (
            sem(s) for s in ("turn_done", "diff_t_ready", "attended", "o_ready"))
        conv_step, conv_done = sem("conv_step"), sem("conv_done")
        y_hi_done, y_lo_done = sem("y_hi_done"), sem("y_lo_done")
        p_hi_done, p_lo_done = sem("p_hi_done"), sem("p_lo_done")
        sigmoid_done, gated = sem("sigmoid_done"), sem("gated")

        def tile(t, k, n=1):
            return t[:, k * T:(k + n) * T]

        def dyn(t, k):
            return t[:, bass.ds(k * T, T)]

        def inner(l, f, part, t):
            return (2 * l + f) * sum(PARTS) + sum(PARTS[:part]) + t

        def ahead(turn, j):
            return (turn, j + 3) if j < 1 else (turn + 1, j - 1)

        block = ctx.enter_context(nc.Block())

        @block.sync
        def _(sp):
            def load(slot, src):
                sp.dma_start(raw[slot][:, 0:src.shape[-1]], src).then_inc(raw_loaded[slot], 16)

            def load_section(l, at, count, source):
                with sp.Fori(0, count // SLOTS) as i:
                    for j in range(SLOTS):
                        sp.wait_ge(lo_split, l * CHUNKS + at + SLOTS * i + j - SLOTS + 1)
                        load(j, source(SLOTS * i + j))

            sp.dma_start(vecs[:, :], vec_in).then_inc(consts_loaded, 16)
            sp.dma_start(lam_vecs[:, :], lam_in.partition_broadcast(P)).then_inc(consts_loaded, 16)
            sp.sem_inc(p_loaded, 16)
            for semaphore in raw_loaded:
                sp.sem_inc(semaphore, 16 * CHUNKS // SLOTS)
            with sp.Fori(1, LAYERS + 1) as l:
                for f in range(2):
                    at, done = AT_FFN[f], 0
                    for part, tiles in enumerate(PARTS):
                        load_section(l, at, 2 * tiles, lambda n: w_gu[l - 1, f, 2 * done + n, :, :])
                        at += 2 * tiles
                        load_section(l, at, KD, lambda n: w_down[part][l - 1, f, n, :, :])
                        at += KD
                        done += tiles
                        if f == 0 and part == 0:
                            sp.wait_ge(p_lo_done, l)
                            sp.wait_ge(diff_ready, l * 4 * HEADS)
                            sp.dma_start(p_raw[:, :], p_in[l - 1, :, :]).then_inc(p_loaded, 16)
                    if f == 0:
                        load_section(l, AT_MIX, len(MIX), lambda n: w_mix[l - 1, n, :, :])
                        load_section(l, AT_OUT, KD, lambda n: w_out[l - 1, n, :, :])
                load_section(l, AT_PLE, KD, lambda n: w_ple[l - 1, n, :, :])
            sp.wait_ge(lo_split, (LAYERS + 1) * CHUNKS - SLOTS + 1)
            sp.sem_inc(raw_loaded[0], 16)
            for k in range(KD):
                sp.wait_ge(x_done, LAYERS * KD + k + 1)
                sp.dma_start(out[:, k * T:(k + 1) * T], tile(x, k)).then_inc(out_stored, 16)
            sp.wait_ge(out_stored, 16 * KD)

        @block.gpsimd
        def _(pool):
            pool.memset(ident[:, :], 0.0).then_inc(zeroed, 1)
            pool.memset(causal[:, :], 0.0).then_inc(zeroed, 1)
            pool.memset(ones2[:, :], 1.0).then_inc(consts_ready, 1)
            pool.memset(halves[:, :], 0.0).then_inc(zeroed, 1)
            pool.memset(eps[:, :], EPS).then_inc(consts_ready, 1)
            pool.memset(u_pad[:, 0:2], 0.0).then_inc(consts_ready, 1)
            pool.wait_ge(zeroed, 3)
            pool.wait_ge(consts_ready, 3)
            pool.memset(halves[0:QK, 0:1], 1.0).then_inc(consts_ready, 1)
            pool.wait_ge(consts_ready, 4)
            pool.memset(halves[QK:P, 1:2], 1.0).then_inc(consts_ready, 1)
            pool.wait_ge(consts_ready, 5)
            pool.affine_select(out=ident[:, :], in_=ident[:, :], compare_op=ALU.not_equal, fill=1.0,
                               base=0, pattern=[[-1, P]], channel_multiplier=1).then_inc(consts_ready, 1)
            pool.affine_select(out=causal[:, :], in_=causal[:, :], compare_op=ALU.is_ge, fill=-1e30,
                               base=0, pattern=[[-1, P]], channel_multiplier=1).then_inc(consts_ready, 1)
        CONSTS = 7

        @block.tensor
        def _(pe):
            def passes(to, k, slot, right_hi, right_lo, start, stop):
                hi, lo = w_hi[slot][:, k * P:(k + 1) * P], w_lo[slot][:, k * P:(k + 1) * P]
                pe.matmul(to, hi, right_lo, start=start, stop=False)
                pe.matmul(to, hi, right_hi, start=False, stop=False)
                return pe.matmul(to, lo, right_hi, start=False, stop=stop)

            def group(l, turn, j, right, blocks, tile_ready=None, hooks=(), last=None):
                n = l * CHUNKS + 4 * turn + j
                pe.wait_ge(lo_split, n + 1)
                pe.wait_ge(drained, n - 1)
                hooks = list(hooks)
                for k in range(blocks):
                    if tile_ready:
                        tile_ready(k)
                    ins = passes(acc[j % 2][:, :], k, j, tile(right[0], k), tile(right[1], k),
                                 k == 0, k == blocks - 1)
                    if k == blocks - 1:
                        if last:
                            ins = last()
                        ins.then_inc(group_done, 1)
                    while hooks and hooks[0][0] <= k:
                        hooks.pop(0)[1]()

            def column_sums(nu, of, which, ready, count):
                pe.wait_ge(ready, count)
                pe.wait_ge(std_done, nu)
                for j in range(4):
                    ins = pe.matmul(sums[:, 2 * j:2 * j + 2], of[:, j * P:(j + 1) * P], which[:, :],
                                    start=True, stop=True)
                ins.then_inc(sums_done, 1)

            def spread_factors(nu):
                pe.wait_ge(wide_done, nu + 1)
                pe.wait_ge(norm_used, nu)
                for j in range(4):
                    ins = pe.transpose(spread[:, j * P:(j + 1) * P], inv_wide[:, j * P:(j + 1) * P], ident[:, :])
                ins.then_inc(spread_done, 1)

            def resid_hooks(l, s):
                nu = l * NORMS + RESID_AT[s]
                return ([(KD - 1,
                          lambda: column_sums(nu, square_sum, ones2, sq_x_added, (l * RESID + s + 1) * (KD - 1)))],
                        [(5, lambda: spread_factors(nu))])

            def h_ready(l, s):
                return lambda k: pe.wait_ge(h_lo_done, (l * RESID + s) * KD + k + 1)

            def section(l, turn, turns, right, blocks, ready=None, hooks=((), ())):
                if ready:
                    for j in range(4):
                        group(l, turn, j, right, blocks, tile_ready=ready if j == 0 else None,
                              hooks=hooks[j] if j < 2 else ())
                with pe.Fori(1 if ready else 0, turns) as i:
                    for j in range(4):
                        group(l, turn + i, j, right, blocks)

            def ffn(l, f):
                turn = AT_FFN[f] // 4
                for part, tiles in enumerate(PARTS):
                    if part == 0:
                        section(l, turn, tiles // 2, (h_hi, h_lo), KD, ready=h_ready(l, 2 * f),
                                hooks=resid_hooks(l, 2 * f))
                    else:
                        section(l, turn, tiles // 2, (h_hi, h_lo), KD)
                    turn += tiles // 2
                    section(l, turn, KD // 4, (a_hi, a_lo), tiles,
                            ready=lambda k: pe.wait_ge(a_lo_done, inner(l, f, part, k) + 1))
                    turn += KD // 4

            def mix_task(l, task, head):
                h, i = head if isinstance(head, tuple) else (head, 0)
                c = l * HEADS + h
                e = 4 * c + i
                s = h % 2
                if task.endswith("_sum"):
                    at = NORM_AT[task[0], h]
                    column_sums(l * NORMS + at, square, ones2 if task == "o_sum" else halves,
                                square_done, l * 4 * HEADS + at - 2 + 1)
                elif task.endswith("_spread"):
                    spread_factors(l * NORMS + NORM_AT[task[0], h])
                elif task == "v_turn":
                    pe.wait_ge(drained, l * CHUNKS + AT_MIX + MIX.index(("v", h)) + 1)
                    pe.wait_ge(o_ready, c)
                    for j in range(4):
                        ins = pe.transpose(values[:, j * P:(j + 1) * P], v_t[:, j * P:(j + 1) * P], ident[:, :])
                    ins.then_inc(v_turned, 1)
                elif task == "score":
                    pe.wait_ge(norm_used, l * NORMS + NORM_AT["k", h] + 1)
                    pe.wait_ge(exp_done, e)
                    n = P * (i + 1)
                    for m in range(2):
                        rows = slice(QK * m, QK * (m + 1))
                        ins = pe.matmul(scores[:, m * T:m * T + n], q_t[s][rows, i * P:(i + 1) * P],
                                        k_t[s][rows, 0:n], start=True, stop=True)
                    ins.then_inc(scores_done, 1)
                elif task == "turn":
                    pe.wait_ge(diff_ready, e + 1)
                    pe.wait_ge(diff_t_ready, e)
                    for j in range(i + 1):
                        at = diff_at[i] + j * P
                        ins = pe.transpose(turned[:, j * P:(j + 1) * P], diff[:, at:at + P], ident[:, :])
                    ins.then_inc(turn_done, 1)
                elif task == "attend":
                    pe.wait_ge(v_rows_ready, c + 1)
                    pe.wait_ge(diff_t_ready, 4 * c + 4)
                    for j in range(4):
                        ins = pe.matmul(values[:, j * P:T], v_rows[s][:, j * P:(j + 1) * P],
                                        diff_t[:, j * T + j * P:(j + 1) * T], start=j == 0, stop=j == 3)
                    ins.then_inc(attended, 1)

            def mixer_hooks(l, c):
                return [(k, lambda task=task, head=head: mix_task(l, task, head)) for k, task, head in HOOKS.get(c, [])]

            def mixer(l):
                resid = resid_hooks(l, 1)
                for c in range(len(MIX)):
                    group(l, (AT_MIX + c) // 4, c % 4, (h_hi, h_lo), KD,
                          tile_ready=h_ready(l, 1) if c == 0 else None,
                          hooks=resid[c] if c < 2 else mixer_hooks(l, c))

            def project(l):
                def y_ready(k):
                    pe.wait_ge(y_lo_done, l * 2 * HEADS + k + 1)
                turn, early = AT_OUT // 4, KD - 2

                def block_of(j, k):
                    return passes(acc[j][:, :], k, j, tile(a_hi, k), tile(a_lo, k), k == 0, k == KD - 1)

                for j in range(2):
                    n = l * CHUNKS + AT_OUT + j
                    pe.wait_ge(lo_split, n + 1)
                    pe.wait_ge(drained, n - 1)
                    hooks = mixer_hooks(l, len(MIX) + j)
                    for k in range(early):
                        if j == 0:
                            y_ready(k)
                        block_of(j, k)
                        while hooks and (hooks[0][0] <= k or k == early - 1):
                            hooks.pop(0)[1]()
                for k in range(early, KD):
                    y_ready(k)
                    for j in range(2):
                        ins = block_of(j, k)
                        if k == KD - 1:
                            ins.then_inc(group_done, 1)
                for j in range(2, 4):
                    group(l, turn, j, (a_hi, a_lo), KD)
                with pe.Fori(1, KD // 4) as i:
                    for j in range(4):
                        group(l, turn + i, j, (a_hi, a_lo), KD)

            def embed(l):
                def both(turn, j, **how):
                    m = 4 * (turn - AT_PLE // 4) + j

                    def project_embedding():
                        pe.wait_ge(gated, l * KD + m - 1)
                        if isinstance(m, int) and m == 0:
                            pe.wait_ge(exp_done, (l + 1) * 4 * HEADS)
                            pe.wait_ge(p_lo_done, l + 1)
                        for k in range(KP):
                            ins = passes(scores[:, (j % 2) * T:(j % 2 + 1) * T], KD + k, j, tile(p_hi, k), tile(p_lo, k),
                                         k == 0, k == KP - 1)
                        return ins
                    group(l, turn, j, (h_hi, h_lo), KD, last=project_embedding, **how)
                resid = resid_hooks(l, 3)
                for j in range(4):
                    both(AT_PLE // 4, j, tile_ready=h_ready(l, 3) if j == 0 else None, hooks=resid[j] if j < 2 else ())
                with pe.Fori(1, KD // 4) as i:
                    for j in range(4):
                        both(AT_PLE // 4 + i, j)

            pe.wait_ge(consts_ready, CONSTS)
            for semaphore, count in (
                (group_done, CHUNKS),
                (sums_done, NORMS),
                (spread_done, NORMS),
                (v_turned, HEADS),
                (scores_done, 4 * HEADS),
                (turn_done, 4 * HEADS),
                (attended, HEADS),
            ):
                pe.sem_inc(semaphore, count)
            with pe.Fori(1, LAYERS + 1) as l:
                ffn(l, 0)
                mixer(l)
                project(l)
                ffn(l, 1)
                embed(l)

        @block.scalar
        def _(act):
            def split(l, turn, j, blocks):
                w = blocks * P
                act.wait_ge(raw_loaded[j], 16 * (l * (CHUNKS // SLOTS) + turn + 1))
                act.activation(w_hi[j][:, 0:w], raw[j][:, 0:w], ACT.Copy).then_inc(hi_split, 1)

            def result(l, turn, j):
                act.wait_ge(group_done, l * CHUNKS + 4 * turn + j + 1)

            def square_tile(l, s, k):
                if k == 0:
                    act.wait_ge(std_done, l * NORMS + RESID_AT[s])
                elif k > 2:
                    act.wait_ge(sq_x_added, (l * RESID + s) * (KD - 1) + k - 2)
                to = square_sum if k == 0 else square_x[k % 2]
                act.activation(to[:, :], tile(x, k), ACT.Square).then_inc(sq_x_done, 1)

            def hi_tile(k, gain_at):
                act.activation(tile(h_hi, k), tile(x, k), ACT.Copy,
                               scale=gain[:, gain_at + k:gain_at + k + 1]).then_inc(h_hi_done, 1)

            def norm_tile(l, s, k, gain_at):
                hi_tile(k, gain_at)
                square_tile(l, s, k)

            def take_std(nu, width):
                act.wait_ge(sums_done, nu + 1)
                act.wait_ge(inv_done, nu)
                act.activation(std[:, :], sums[:, 0:8], ACT.Sqrt, scale=1.0 / width,
                               bias=eps[:, 0:1]).then_inc(std_done, 1)

            def resid_norm(l, s):
                nu = l * NORMS + RESID_AT[s]
                take_std(nu, D)
                act.wait_ge(spread_done, nu + 1)
                act.activation(rstd[:, :], spread[:, :], ACT.Copy).then_inc(norm_used, 1)

            def ffn(l, f):
                turn = AT_FFN[f] // 4
                for part, tiles in enumerate(PARTS):
                    def two_tiles(i, blocks_next=KD, norm=False):
                        for half in range(2):
                            t = inner(l, f, part, 2 * i + half)
                            gate, up = 2 * half, 2 * half + 1
                            result(l, turn + i, gate)
                            if norm and half == 0:
                                resid_norm(l, 2 * f)
                            else:
                                split(l, *ahead(turn + i, gate), blocks_next if half else KD)
                            act.wait_ge(drained, l * CHUNKS + 4 * (turn + i) + gate + 1)
                            act.wait_ge(inner_done, t)
                            act.activation(tmp_b[:, :], tmp_a[:, :], ACT.Silu).then_inc(silu_done, 1)
                            if norm and half == 0:
                                split(l, *ahead(turn + i, gate), KD)
                            result(l, turn + i, up)
                            act.wait_ge(inner_done, t + 1)
                            act.activation(dyn(a_hi, 2 * i + half), tmp_d[:, :], ACT.Copy).then_inc(a_hi_done, 1)
                            split(l, *ahead(turn + i, up), blocks_next)

                    if part == 0:
                        two_tiles(0, norm=True)
                    with act.Fori(1 if part == 0 else 0, tiles // 2 - 1) as i:
                        two_tiles(i)
                    two_tiles(tiles // 2 - 1, blocks_next=tiles)
                    turn += tiles // 2
                    last_part = part == len(PARTS) - 1
                    after = PLE_BLOCKS if last_part and f else KD
                    for m in range(KD):
                        at, j = turn + m // 4, m % 4
                        result(l, at, j)
                        if last_part:
                            act.wait_ge(drained, l * CHUNKS + 4 * at + j + 1)
                            norm_tile(l, 2 * f + 1, m, G_MIX if f == 0 else G_PLE)
                        split(l, *ahead(at, j), tiles if m < KD - 3 else after)
                        if f == 0 and part == 1 and m == 1:
                            act.wait_ge(p_loaded, 16 * l + 16)
                            act.activation(p_hi[:, :], p_raw[:, :], ACT.Copy).then_inc(p_hi_done, 1)
                    turn += KD // 4

            def take_square(l, kind, h, of):
                act.wait_ge(sums_done, l * NORMS + NORM_AT[kind, h])
                act.activation(square[:, :], of[:, :], ACT.Square).then_inc(square_done, 1)

            def mix_task(l, task, head):
                h, i = head if isinstance(head, tuple) else (head, 0)
                c = l * HEADS + h
                e = 4 * c + i
                s = h % 2
                if task.endswith("_sum"):
                    take_std(l * NORMS + NORM_AT[task[0], h], P if task == "o_sum" else QK)
                elif task in ("o_spread", "c_spread"):
                    act.wait_ge(norm_used, l * NORMS + NORM_AT[task[0], h] + 1)
                    act.activation(tile(a_hi, Y_AT[task[0], h]), tmp_d[:, :],
                                   ACT.Copy).then_inc(y_hi_done, 1)
                elif task == "v_turn":
                    act.wait_ge(v_turned, c + 1)
                    act.activation(v_rows[s][:, :], values[:, :], ACT.Copy).then_inc(v_rows_ready, 1)
                elif task == "score":
                    n = P * (i + 1)
                    act.wait_ge(max_ready, e + 1)
                    act.wait_ge(diff_ready, e)
                    if (h, i) == (0, 0):
                        act.wait_ge(p_lo_done, l + 1)
                    for m in range(2):
                        ins = act.activation(exps[:, m * T:m * T + n], scores[:, m * T:m * T + n], ACT.Exp,
                                             scale=QK ** -0.5, bias=row_max[:, m:m + 1],
                                             accum_out=row_sum[:, m:m + 1])
                    ins.then_inc(exp_done, 1)
                elif task == "turn":
                    act.wait_ge(turn_done, e + 1)
                    act.wait_ge(attended, c)
                    act.activation(diff_t[:, :].rearrange("p (j q) -> p j q", q=T)[:, 0:i + 1, i * P:(i + 1) * P],
                                   turned[:, 0:(i + 1) * P].rearrange("p (j q) -> p j q", q=P),
                                   ACT.Copy).then_inc(diff_t_ready, 1)
                elif task == "attend":
                    act.wait_ge(attended, c + 1)
                    if h:
                        act.wait_ge(norm_used, l * NORMS + NORM_AT["o", h - 1] + 1)
                    act.activation(o_t[:, :], values[:, :], ACT.Copy).then_inc(o_ready, 1)
                    act.wait_ge(o_ready, c + 1)
                    take_square(l, "o", h, o_t)

            def mixer(l):
                for c, (kind, h) in enumerate(MIX):
                    turn, j = (AT_MIX + c) // 4, c % 4
                    result(l, turn, j)
                    if c == 0:
                        resid_norm(l, 1)
                    if kind in "qk":
                        act.wait_ge(drained, l * CHUNKS + AT_MIX + c + 1)
                        take_square(l, kind, h, (q_t if kind == "q" else k_t)[h % 2])
                    if kind == "b":
                        act.wait_ge(conv_done, l * HEADS + h + 1)
                        take_square(l, "c", h, tmp_c)
                    tasks = HOOKS.get(c + 1, []) + (HOOKS.get(c + 2, []) if c == len(MIX) - 1 else [])
                    for at, task, head in tasks:
                        if at < SPLIT_BEFORE[c]:
                            mix_task(l, task, head)
                    split(l, *ahead(turn, j), KD)
                    for at, task, head in tasks:
                        if at >= SPLIT_BEFORE[c]:
                            mix_task(l, task, head)

            def project(l):
                for m in range(KD):
                    turn, j = (AT_OUT + m) // 4, m % 4
                    result(l, turn, j)
                    act.wait_ge(drained, l * CHUNKS + AT_OUT + m + 1)
                    norm_tile(l, 2, m, G_FFN2)
                    split(l, *ahead(turn, j), KD)

            def embed(l):
                for m in range(KD):
                    turn, j = (AT_PLE + m) // 4, m % 4
                    result(l, turn, j)
                    if m == 0:
                        resid_norm(l, 3)
                    else:
                        next_square(l, m - 1)
                    act.wait_ge(drained, l * CHUNKS + AT_PLE + m + 1)
                    act.wait_ge(gated, l * KD + m)
                    act.activation(tmp_b[:, :], tmp_a[:, :], ACT.Sigmoid).then_inc(sigmoid_done, 1)
                    if m < KD - 3:
                        split(l, *ahead(turn, j), PLE_BLOCKS)
                    elif m == KD - 3:
                        split(l, *ahead(turn, j), KD)

            def next_square(l, k):
                act.wait_ge(x_done, l * KD + k + 1)
                square_tile(l + 1, 0, k)

            for k in range(KD):
                act.dma_start(tile(x, k), x_in[:, k * T:(k + 1) * T]).then_inc(x_loaded[k], 16)
            act.wait_ge(setup_step, 2)
            act.activation(lam_exp[:, :], lam_sum[:, :], ACT.Exp).then_inc(lam_exp_ready, 1)
            act.wait_ge(consts_ready, CONSTS)
            for semaphore, count in (
                (hi_split, CHUNKS),
                (h_hi_done, RESID * KD),
                (sq_x_done, RESID * KD),
                (square_done, 4 * HEADS),
                (std_done, NORMS),
                (norm_used, RESID),
                (silu_done, 2 * sum(PARTS)),
                (a_hi_done, 2 * sum(PARTS)),
                (v_rows_ready, HEADS),
                (exp_done, 4 * HEADS),
                (diff_t_ready, 4 * HEADS),
                (o_ready, HEADS),
                (y_hi_done, 2 * HEADS),
                (p_hi_done, 1),
                (sigmoid_done, KD),
                (gain_ready, 2),
            ):
                act.sem_inc(semaphore, count)
            for k in range(KD - 1):
                act.wait_ge(x_loaded[k], 16)
                square_tile(1, 0, k)
                if k == 1:
                    split(1, 0, 0, KD)
            act.wait_ge(x_loaded[KD - 1], 16)
            act.wait_ge(setup_step, 2 + 2 * LAYERS)
            act.wait_ge(gain_scaled, LAYERS)
            with act.Fori(1, LAYERS + 1) as l:
                act.wait_ge(h_lo_done, l * RESID * KD)
                act.activation(gain[:, :], vecs[:, bass.ds((l - 1) * GAINS, GAINS)], ACT.Copy).then_inc(gain_ready, 1)
                act.activation(neg_lam_now[:, :], neg_lam[:, bass.ds(l - 1, 1)], ACT.Copy).then_inc(gain_ready, 1)
                act.wait_ge(gain_ready, 2 * l + 2)
                act.wait_ge(group_done, l * CHUNKS)
                for k in range(KD):
                    act.wait_ge(x_done, (l - 1) * KD + k + 1)
                    hi_tile(k, G_FFN1)
                square_tile(l, 0, KD - 1)
                split(l, 0, 1, KD)
                split(l, 0, 2, KD)
                ffn(l, 0)
                mixer(l)
                project(l)
                ffn(l, 1)
                embed(l)

        @block.vector
        def _(dve):
            def split(l, turn, j, blocks):
                w = blocks * P
                dve.wait_ge(hi_split, l * CHUNKS + 4 * turn + j + 1)
                dve.wait_ge(raw_loaded[j], 16 * (l * (CHUNKS // SLOTS) + turn + 1))
                dve.tensor_tensor(w_lo[j][:, 0:w], raw[j][:, 0:w],
                                  w_hi[j][:, 0:w].bitcast(f32), ALU.subtract).then_inc(lo_split, 1)

            def result(l, turn, j):
                dve.wait_ge(group_done, l * CHUNKS + 4 * turn + j + 1)

            def scaled(l, turn, j, to):
                dve.tensor_tensor(to, acc[j % 2][:, :], rstd[:, :], ALU.mult).then_inc(drained, 1)
                return l * CHUNKS + 4 * turn + j + 1

            def into_x(l, turn, j, m, factor):
                dve.scalar_tensor_tensor(out=tile(x, m), in0=acc[j % 2][:, :], scalar=factor, in1=tile(x, m),
                                         op0=ALU.mult, op1=ALU.add).then_inc(drained, 1)

            def add_squares(l, s, k):
                if k:
                    dve.wait_ge(sq_x_done, (l * RESID + s) * KD + k + 1)
                    if k > 1:
                        dve.wait_ge(sq_x_added, (l * RESID + s) * (KD - 1) + k - 1)
                    dve.tensor_tensor(square_sum[:, :], square_sum[:, :], square_x[k % 2][:, :],
                                      ALU.add).then_inc(sq_x_added, 1)

            def lo_tile(l, s, k, gain_at):
                dve.wait_ge(h_hi_done, (l * RESID + s) * KD + k + 1)
                dve.scalar_tensor_tensor(out=tile(h_lo, k), in0=tile(x, k),
                                         scalar=gain[:, gain_at + k:gain_at + k + 1],
                                         in1=tile(h_hi, k).bitcast(f32), op0=ALU.mult,
                                         op1=ALU.subtract).then_inc(h_lo_done, 1)

            def norm_tile(l, s, k, gain_at):
                lo_tile(l, s, k, gain_at)
                add_squares(l, s, k)

            def take_inv(nu):
                dve.wait_ge(std_done, nu + 1)
                dve.wait_ge(wide_done, nu)
                dve.reciprocal(inv[:, :], std[:, :]).then_inc(inv_done, 1)
                dve.wait_ge(inv_done, nu + 1)
                dve.wait_ge(spread_done, nu)
                dve.tensor_copy(inv_wide[:, :].rearrange("p (c d) -> p c d", d=QK),
                                inv[:, :].unsqueeze(2).broadcast_to([P, 8, QK])).then_inc(wide_done, 1)

            def resid_norm(l, s):
                take_inv(l * NORMS + RESID_AT[s])
                dve.wait_ge(norm_used, l * NORMS + RESID_AT[s] + 1)

            def ffn(l, f):
                turn = AT_FFN[f] // 4
                for part, tiles in enumerate(PARTS):
                    def two_tiles(i, blocks_next=KD, norm=False):
                        for half in range(2):
                            t = inner(l, f, part, 2 * i + half)
                            gate, up = 2 * half, 2 * half + 1
                            result(l, turn + i, gate)
                            if norm and half == 0:
                                resid_norm(l, 2 * f)
                            dve.wait_ge(silu_done, t)
                            scaled(l, turn + i, gate, tmp_a[:, :])
                            split(l, *ahead(turn + i, gate), blocks_next if half else KD)
                            result(l, turn + i, up)
                            count = scaled(l, turn + i, up, tmp_c[:, :])
                            dve.wait_ge(drained, count)
                            dve.wait_ge(silu_done, t + 1)
                            dve.wait_ge(a_hi_done, t)
                            dve.tensor_tensor(tmp_d[:, :], tmp_b[:, :], tmp_c[:, :], ALU.mult).then_inc(inner_done, 1)
                            dve.wait_ge(inner_done, t + 1)
                            dve.wait_ge(a_hi_done, t + 1)
                            dve.tensor_tensor(dyn(a_lo, 2 * i + half), tmp_d[:, :],
                                              dyn(a_hi, 2 * i + half).bitcast(f32), ALU.subtract).then_inc(a_lo_done, 1)
                            split(l, *ahead(turn + i, up), blocks_next)

                    if part == 0:
                        two_tiles(0, norm=True)
                    with dve.Fori(1 if part == 0 else 0, tiles // 2 - 1) as i:
                        two_tiles(i)
                    two_tiles(tiles // 2 - 1, blocks_next=tiles)
                    turn += tiles // 2
                    last_part = part == len(PARTS) - 1
                    after = PLE_BLOCKS if last_part and f else KD
                    for m in range(KD):
                        at, j = turn + m // 4, m % 4
                        result(l, at, j)
                        into_x(l, at, j, m, 0.5)
                        if last_part:
                            dve.wait_ge(drained, l * CHUNKS + 4 * at + j + 1)
                            norm_tile(l, 2 * f + 1, m, G_MIX if f == 0 else G_PLE)
                        split(l, *ahead(at, j), tiles if m < KD - 3 else after)
                        if f == 0 and part == 1 and m == 1:
                            dve.wait_ge(p_hi_done, l + 1)
                            dve.tensor_tensor(p_lo[:, :], p_raw[:, :], p_hi[:, :].bitcast(f32),
                                              ALU.subtract).then_inc(p_lo_done, 1)
                    turn += KD // 4

            def link(l, h, step, ins):
                ins.then_inc(conv_step, 1)
                dve.wait_ge(conv_step, (l * HEADS + h) * CONV_STEPS + step + 1)

            def convolve(l, h):
                taps = [gain[:, G_CW + 4 * t + h:G_CW + 4 * t + h + 1] for t in range(3)]
                link(l, h, 0, dve.tensor_tensor(u_pad[:, 2:T + 2], tmp_a[:, :], tmp_b[:, :], ALU.mult))
                link(l, h, 1, dve.tensor_scalar(tmp_c[:, :], u_pad[:, 2:T + 2], taps[2],
                                                gain[:, G_CB + h:G_CB + h + 1], ALU.mult, ALU.add))
                for t in (1, 0):
                    link(l, h, 3 - t, dve.scalar_tensor_tensor(out=tmp_c[:, :], in0=u_pad[:, t:T + t], scalar=taps[t],
                                                               in1=tmp_c[:, :], op0=ALU.mult, op1=ALU.add))

            def norm_out(l, kind, h, of, gain_at):
                y = l * 2 * HEADS + Y_AT[kind, h]
                k = Y_AT[kind, h]
                nu = l * NORMS + NORM_AT[kind, h]
                dve.wait_ge(spread_done, nu + 1)
                dve.wait_ge(y_hi_done, y)
                if kind == "o":
                    dve.wait_ge(o_ready, l * HEADS + h + 1)
                else:
                    dve.wait_ge(conv_done, l * HEADS + h + 1)
                dve.scalar_tensor_tensor(out=tmp_d[:, :], in0=of[:, :], scalar=gain_at, in1=spread[:, :],
                                         op0=ALU.mult, op1=ALU.mult).then_inc(norm_used, 1)
                dve.wait_ge(norm_used, nu + 1)
                dve.wait_ge(y_hi_done, y + 1)
                dve.tensor_tensor(tile(a_lo, k), tmp_d[:, :], tile(a_hi, k).bitcast(f32),
                                  ALU.subtract).then_inc(y_lo_done, 1)

            def row_maxima(l, h, i):
                e = 4 * (l * HEADS + h) + i
                n = P * (i + 1)
                both = scores[:, :].rearrange("p (m k) -> p m k", m=2)
                dve.wait_ge(scores_done, e + 1)
                dve.wait_ge(exp_done, e)
                dve.tensor_tensor(both[:, :, i * P:n], both[:, :, i * P:n],
                                  causal[:, :].unsqueeze(1).broadcast_to([P, 2, P]), ALU.add).then_inc(masked, 1)
                dve.wait_ge(masked, e + 1)
                dve.tensor_reduce(row_top[:, :], both[:, :, 0:n], AX.X, ALU.max).then_inc(max_done, 1)
                dve.wait_ge(max_done, e + 1)
                dve.tensor_scalar(row_max[:, :], row_top[:, :], -(QK ** -0.5), None, ALU.mult).then_inc(max_ready, 1)

            def weigh(l, h, i):
                e = 4 * (l * HEADS + h) + i
                n = P * (i + 1)
                dve.wait_ge(exp_done, e + 1)
                dve.reciprocal(row_inv[:, :], row_sum[:, :]).then_inc(inv_step, 1)
                dve.wait_ge(inv_step, 2 * e + 1)
                dve.tensor_tensor(row_inv[:, 1:2], row_inv[:, 1:2], neg_lam_now[:, :], ALU.mult).then_inc(inv_step, 1)
                dve.wait_ge(inv_step, 2 * e + 2)
                dve.wait_ge(turn_done, e - 3)
                to = diff[:, diff_at[i]:diff_at[i] + n]
                dve.tensor_scalar(to, exps[:, 0:n], row_inv[:, 0:1], None, ALU.mult).then_inc(diff_step, 1)
                dve.wait_ge(diff_step, e + 1)
                dve.scalar_tensor_tensor(out=to, in0=exps[:, T:T + n], scalar=row_inv[:, 1:2], in1=to,
                                         op0=ALU.mult, op1=ALU.add).then_inc(diff_ready, 1)

            def mix_task(l, task, head):
                h, i = head if isinstance(head, tuple) else (head, 0)
                if task.endswith("_sum"):
                    take_inv(l * NORMS + NORM_AT[task[0], h])
                elif task in ("q_spread", "k_spread"):
                    of, g = (q_t[h % 2], G_Q) if task == "q_spread" else (k_t[h % 2], G_K)
                    dve.wait_ge(spread_done, l * NORMS + NORM_AT[task[0], h] + 1)
                    dve.scalar_tensor_tensor(out=of[:, :], in0=of[:, :], scalar=gain[:, g:g + 1],
                                             in1=spread[:, :], op0=ALU.mult, op1=ALU.mult).then_inc(norm_used, 1)
                elif task == "o_spread":
                    norm_out(l, "o", h, o_t, gain[:, G_O:G_O + 1])
                elif task == "c_spread":
                    norm_out(l, "c", h, tmp_c, gain[:, G_CN + h:G_CN + h + 1])
                elif task == "score":
                    row_maxima(l, h, i)
                elif task == "weigh":
                    weigh(l, h, i)

            def mixer(l):
                for c, (kind, h) in enumerate(MIX):
                    turn, j = (AT_MIX + c) // 4, c % 4
                    result(l, turn, j)
                    if c == 0:
                        resid_norm(l, 1)
                    if kind in "qk":
                        dve.wait_ge(scores_done, 4 * (l * HEADS + h - 1))
                    if kind == "v":
                        dve.wait_ge(v_turned, l * HEADS + h)
                    to = {"q": q_t[h % 2], "k": k_t[h % 2], "v": v_t, "c": tmp_a, "h": tmp_b, "b": tmp_b}[kind]
                    count = scaled(l, turn, j, to[:, :])
                    if kind == "h":
                        dve.wait_ge(drained, count)
                        convolve(l, h)
                    if kind == "b":
                        dve.wait_ge(drained, count)
                        dve.tensor_tensor(tmp_c[:, :], tmp_c[:, :], tmp_b[:, :], ALU.mult).then_inc(conv_done, 1)
                    tasks = HOOKS.get(c + 1, []) + (HOOKS.get(c + 2, []) if c == len(MIX) - 1 else [])
                    for at, task, head in tasks:
                        if at < SPLIT_BEFORE[c]:
                            mix_task(l, task, head)
                    split(l, *ahead(turn, j), KD)
                    for at, task, head in tasks:
                        if at >= SPLIT_BEFORE[c]:
                            mix_task(l, task, head)

            def project(l):
                for m in range(KD):
                    turn, j = (AT_OUT + m) // 4, m % 4
                    result(l, turn, j)
                    into_x(l, turn, j, m, 1.0)
                    dve.wait_ge(drained, l * CHUNKS + AT_OUT + m + 1)
                    norm_tile(l, 2, m, G_FFN2)
                    split(l, *ahead(turn, j), KD)

            def embed(l):
                for m in range(KD):
                    turn, j = (AT_PLE + m) // 4, m % 4
                    result(l, turn, j)
                    if m == 0:
                        resid_norm(l, 3)
                    dve.wait_ge(sigmoid_done, l * KD + m)
                    scaled(l, turn, j, tmp_a[:, :])
                    if m:
                        add_squares(l + 1, 0, m - 1)
                    dve.wait_ge(sigmoid_done, l * KD + m + 1)
                    dve.tensor_tensor(tmp_c[:, :], scores[:, (j % 2) * T:(j % 2 + 1) * T], tmp_b[:, :],
                                      ALU.mult).then_inc(gated, 1)
                    dve.wait_ge(gated, l * KD + m + 1)
                    dve.tensor_tensor(tile(x, m), tile(x, m), tmp_c[:, :], ALU.add).then_inc(x_done, 1)
                    if m < KD - 3:
                        split(l, *ahead(turn, j), PLE_BLOCKS)
                    elif m == KD - 3:
                        split(l, *ahead(turn, j), KD)

            for semaphore, count in (
                (lo_split, CHUNKS - SLOTS + 1),
                (drained, CHUNKS),
                (x_done, KD),
                (h_lo_done, RESID * KD),
                (sq_x_added, RESID * (KD - 1)),
                (inv_done, NORMS),
                (wide_done, NORMS),
                (norm_used, NORMS - RESID),
                (inner_done, 2 * sum(PARTS)),
                (a_lo_done, 2 * sum(PARTS)),
                (masked, 4 * HEADS),
                (max_done, 4 * HEADS),
                (max_ready, 4 * HEADS),
                (inv_step, 8 * HEADS),
                (diff_step, 4 * HEADS),
                (diff_ready, 4 * HEADS),
                (conv_step, HEADS * CONV_STEPS),
                (conv_done, HEADS),
                (y_lo_done, 2 * HEADS),
                (p_lo_done, 1),
                (gated, KD),
            ):
                dve.sem_inc(semaphore, count)
            dve.wait_ge(consts_loaded, 32)
            pairs = lam_vecs[:, :].rearrange("p (m a d) -> p m a d", a=2, d=QK)
            products = lam_prod[:, :].rearrange("p (m d) -> p m d", d=QK)
            dve.tensor_tensor(products, pairs[:, :, 0, :], pairs[:, :, 1, :], ALU.mult).then_inc(setup_step, 1)
            dve.wait_ge(setup_step, 1)
            dve.tensor_reduce(lam_sum[:, :], products, AX.X, ALU.add).then_inc(setup_step, 1)
            dve.wait_ge(lam_exp_ready, 1)
            for l in range(LAYERS):
                lam, g = neg_lam[:, l:l + 1], vecs[:, l * GAINS + G_O:l * GAINS + G_O + 1]
                dve.tensor_tensor(lam, lam_exp[:, 2 * l + 1:2 * l + 2], lam_exp[:, 2 * l:2 * l + 1],
                                  ALU.subtract).then_inc(setup_step, 1)
                dve.wait_ge(setup_step, 3 + 2 * l)
                dve.tensor_scalar(lam, lam, -lambda_init(l), None, ALU.add).then_inc(setup_step, 1)
                dve.tensor_scalar(g, g, 1.0 - lambda_init(l), None, ALU.mult).then_inc(gain_scaled, 1)
            dve.wait_ge(setup_step, 2 + 2 * LAYERS)
            dve.wait_ge(gain_scaled, LAYERS)
            dve.wait_ge(consts_ready, CONSTS)
            for k in range(KD - 1):
                dve.wait_ge(x_loaded[k], 16)
                add_squares(1, 0, k)
                if k == 1:
                    split(1, 0, 0, KD)
                if k == 3:
                    dve.sem_inc(lo_split, SLOTS - 1)
            dve.wait_ge(x_loaded[KD - 1], 16)
            with dve.Fori(1, LAYERS + 1) as l:
                dve.wait_ge(gain_ready, 2 * l + 2)
                dve.wait_ge(x_done, l * KD)
                dve.wait_ge(group_done, l * CHUNKS)
                for k in range(KD):
                    lo_tile(l, 0, k, G_FFN1)
                add_squares(l, 0, KD - 1)
                split(l, 0, 1, KD)
                split(l, 0, 2, KD)
                ffn(l, 0)
                mixer(l)
                project(l)
                ffn(l, 1)
                embed(l)


def blocked(w, tiles_in):
    lead = w.shape[:-2]
    w = w.reshape(*lead, tiles_in, P, w.shape[-1] // P, P)
    n = len(lead)
    w = w.transpose(*range(n), n + 2, n + 1, n, n + 3)
    return np.ascontiguousarray(w.reshape(*lead, w.shape[n], P, tiles_in * P))


def columns(v):
    return v.reshape(LAYERS, -1, P).transpose(0, 2, 1)


def kernel(**inputs):
    import concourse.bacc as bacc
    from concourse.bass_utils import run_bass_kernel_spmd as run

    a = {name: np.asarray(v) for name, v in inputs.items()}
    arrays = {}
    gate_up = []
    for f in ("ffn1", "ffn2"):
        g, u = (blocked(a[f"{f}_w_{s}"], KD) for s in ("gate", "up"))
        gate_up.append(np.stack([g, u], axis=2).reshape(LAYERS, -1, P, KD * P))
    arrays["w_gu"] = np.stack(gate_up, axis=1)
    row = 0
    for part, tiles in enumerate(PARTS):
        arrays[f"w_down{part}"] = np.stack(
            [blocked(a[f"{f}_w_down"][:, row:row + tiles * P], tiles) for f in ("ffn1", "ffn2")], axis=1)
        row += tiles * P
    w_in = blocked(a["w_in"], KD)
    arrays["w_mix"] = np.stack([w_in[:, COLUMN[kind] + h] for kind, h in MIX], axis=1)
    rows = [h + (HEADS if kind == "c" else 0) for kind, h in Y_AT]
    arrays["w_out"] = blocked(a["w_out"].reshape(LAYERS, KD, P, D)[:, rows].reshape(LAYERS, D, D), KD)
    arrays["w_ple"] = np.concatenate([blocked(a["ple_w_gate"], KD), blocked(a["ple_w_proj"], KP)], axis=-1)
    arrays["x_in"] = a["x"].reshape(T, KD, P).transpose(2, 1, 0).reshape(P, KD * T)
    arrays["p_in"] = a["p"].reshape(LAYERS, T, KP, P).transpose(0, 3, 2, 1).reshape(LAYERS, P, KP * T)
    vec = [columns(a[n]) for n in ("ffn1_norm", "mix_norm", "ffn2_norm", "ple_norm")]
    vec += [columns(np.tile(a[n], (1, 2))) for n in ("q_norm", "k_norm")]
    vec += [columns(a[n]) for n in ("attn_out_norm", "conv_b", "conv_out_norm")]
    vec.append(columns(a["conv_w"]))
    vec = np.concatenate(vec, axis=2)
    arrays["vec_in"] = vec.transpose(1, 0, 2).reshape(P, LAYERS * GAINS)
    arrays["lam_in"] = np.stack([a[f"lambda_{s}"] for s in ("q1", "k1", "q2", "k2")], axis=1).reshape(-1)
    arrays = {name: np.ascontiguousarray(v) for name, v in arrays.items()}

    nc = bacc.Bacc("TRN2", target_bir_lowering=False, num_devices=1)
    dram = {name: nc.dram_tensor(name, v.shape, mybir.dt.from_np(v.dtype), kind="ExternalInput").ap()
            for name, v in arrays.items()}
    out = nc.dram_tensor("out", (P, KD * T), mybir.dt.float32, kind="ExternalOutput").ap()
    downs = [dram.pop(f"w_down{part}") for part in range(len(PARTS))]
    build(nc, w_down=downs, out=out, **dram)
    got = run(nc, [arrays], core_ids=[0]).results[0]["out"]
    return np.ascontiguousarray(got.reshape(P, KD, T).transpose(2, 1, 0)).reshape(1, T, D)
```
